# Optimizing a Trainium2 kernel written in Bass

```python
import math
import jax, jax.numpy as jnp
from jax import lax
import numpy as np

D_MODEL = 2048
BATCH = 1
SEQ = 256
DEPTH = 2

HEAD_DIM = 128
SB_HEADS = D_MODEL // HEAD_DIM
DIL_CONFIGS = ((128, 1), (512, 4), (2048, 16))
N_DIL_GROUPS = len(DIL_CONFIGS)
DIL_HEADS_PER_GROUP = 6
DIL_HEADS = N_DIL_GROUPS * DIL_HEADS_PER_GROUP
D_FF = -(-(8 * D_MODEL) // (3 * 256)) * 256
BLOCK_Q = 128
ROPE_THETA = 10000.0
LN_EPS = 1e-5
DEEPNORM_ALPHA = (2.0 * DEPTH) ** 0.25
DEEPNORM_BETA = (8.0 * DEPTH) ** -0.25
N_SB_LAYERS = (DEPTH + 1) // 2
N_DIL_LAYERS = DEPTH // 2

kernel_name = 'stickbreak_dilated_deepnorm_hybrid'

def layer_norm(x, g, b):
    xf = x.astype(jnp.float32)
    mu = jnp.mean(xf, axis=-1, keepdims=True)
    var = jnp.mean(jnp.square(xf - mu), axis=-1, keepdims=True)
    y = (xf - mu) * lax.rsqrt(var + LN_EPS) * g.astype(jnp.float32) + b.astype(jnp.float32)
    return y.astype(x.dtype)

def rope_tables(seq_len, dim):
    pos = jnp.arange(seq_len, dtype=jnp.float32)
    inv_freq = ROPE_THETA ** (-jnp.arange(0, dim, 2, dtype=jnp.float32) / dim)
    ang = pos[:, None] * inv_freq[None, :]
    return jnp.cos(ang), jnp.sin(ang)

def apply_rope(x, cos, sin):
    xf = x.astype(jnp.float32)
    x1, x2 = jnp.split(xf, 2, axis=-1)
    c = cos[None, :, None, :]
    s = sin[None, :, None, :]
    return jnp.concatenate([x1 * c - x2 * s, x1 * s + x2 * c], axis=-1).astype(x.dtype)

def stick_breaking_attention(q, k, v):
    b, s, h, d = q.shape
    n_blocks = s // BLOCK_Q
    scale = 1.0 / math.sqrt(d)
    kpos = jnp.arange(s)

    def block(i):
        t0 = i * BLOCK_Q
        qb = lax.dynamic_slice_in_dim(q, t0, BLOCK_Q, axis=1)
        z = jnp.einsum('bqhd,bkhd->bhqk', qb, k, preferred_element_type=jnp.float32) * scale
        qpos = t0 + jnp.arange(BLOCK_Q)
        causal = kpos[None, :] < qpos[:, None]
        log_stay = jnp.where(causal, jax.nn.log_sigmoid(-z), 0.0)
        later = lax.cumsum(log_stay, axis=3, reverse=True) - log_stay
        w = jnp.where(causal, jnp.exp(jax.nn.log_sigmoid(z) + later), 0.0)
        o = jnp.einsum('bhqk,bkhd->bqhd', w, v.astype(jnp.float32))
        return o.astype(q.dtype)

    out = lax.map(block, jnp.arange(n_blocks))
    return jnp.moveaxis(out, 0, 1).reshape(b, s, h, d)

def dilated_window_attention(q, k, v, window, dilation):
    b, s, h, d = q.shape
    n_keys = window // dilation + 1
    n_blocks = s // BLOCK_Q
    scale = 1.0 / math.sqrt(d)
    steps = dilation * jnp.arange(n_keys)

    def block(i):
        t0 = i * BLOCK_Q
        qpos = t0 + jnp.arange(BLOCK_Q)
        idx = qpos[:, None] - steps[None, :]
        valid = idx >= 0
        flat = jnp.maximum(idx, 0).reshape(-1)
        kg = jnp.take(k, flat, axis=1).reshape(b, BLOCK_Q, n_keys, h, d)
        vg = jnp.take(v, flat, axis=1).reshape(b, BLOCK_Q, n_keys, h, d)
        qb = lax.dynamic_slice_in_dim(q, t0, BLOCK_Q, axis=1)
        sc = jnp.einsum('bqhd,bqmhd->bhqm', qb, kg, preferred_element_type=jnp.float32) * scale
        sc = jnp.where(valid[None, None], sc, -jnp.inf)
        m = jnp.max(sc, axis=-1, keepdims=True)
        p = jnp.exp(sc - m)
        den = jnp.sum(p, axis=-1)
        o = jnp.einsum('bhqm,bqmhd->bqhd', p, vg.astype(jnp.float32))
        o = o / jnp.transpose(den, (0, 2, 1))[..., None]
        lse = jnp.transpose(m[..., 0] + jnp.log(den), (0, 2, 1))
        return o.astype(q.dtype), lse

    o, lse = lax.map(block, jnp.arange(n_blocks))
    o = jnp.moveaxis(o, 0, 1).reshape(b, s, h, d)
    lse = jnp.moveaxis(lse, 0, 1).reshape(b, s, h)
    return o, lse

def stick_breaking_mixer(x, w_qkv, w_o):
    b, s, _ = x.shape
    qkv = (x @ w_qkv).reshape(b, s, 3, SB_HEADS, HEAD_DIM)
    o = stick_breaking_attention(qkv[:, :, 0], qkv[:, :, 1], qkv[:, :, 2])
    return o.reshape(b, s, SB_HEADS * HEAD_DIM) @ w_o

def dilated_mixer(x, w_qkv, w_o, cos, sin):
    b, s, _ = x.shape
    qkv = (x @ w_qkv).reshape(b, s, 3, N_DIL_GROUPS, DIL_HEADS_PER_GROUP, HEAD_DIM)
    outs, lses = [], []
    for g, (window, dilation) in enumerate(DIL_CONFIGS):
        q = apply_rope(qkv[:, :, 0, g], cos, sin)
        k = apply_rope(qkv[:, :, 1, g], cos, sin)
        o, lse = dilated_window_attention(q, k, qkv[:, :, 2, g], window, dilation)
        outs.append(o)
        lses.append(lse)
    share = jax.nn.softmax(jnp.stack(lses, axis=0), axis=0)
    o = jnp.stack(outs, axis=0) * share[..., None].astype(x.dtype)
    o = jnp.moveaxis(o, 0, 2).reshape(b, s, DIL_HEADS * HEAD_DIM)
    return o @ w_o

def swiglu(x, w_gate_up, w_down):
    gate, up = jnp.split(x @ w_gate_up, 2, axis=-1)
    return (jax.nn.silu(gate) * up) @ w_down

def setup_inputs(seed: int = 0) -> dict:
    key = jax.random.key(seed)
    ks = jax.random.split(key, 12)
    f32 = jnp.float32
    sb_w = SB_HEADS * HEAD_DIM
    dil_w = DIL_HEADS * HEAD_DIM
    sb_col_scale = jnp.concatenate([jnp.ones((2 * sb_w,), f32), jnp.full((sb_w,), DEEPNORM_BETA, f32)])
    dil_col_scale = jnp.concatenate([jnp.ones((2 * dil_w,), f32), jnp.full((dil_w,), DEEPNORM_BETA, f32)])
    x = jax.random.normal(ks[0], (BATCH, SEQ, D_MODEL), f32)
    w_qkv_sb = jax.random.normal(ks[1], (N_SB_LAYERS, D_MODEL, 3 * sb_w), f32) * (D_MODEL ** -0.5) * sb_col_scale
    w_o_sb = jax.random.normal(ks[2], (N_SB_LAYERS, sb_w, D_MODEL), f32) * (sb_w ** -0.5) * DEEPNORM_BETA
    w_qkv_dil = jax.random.normal(ks[3], (N_DIL_LAYERS, D_MODEL, 3 * dil_w), f32) * (D_MODEL ** -0.5) * dil_col_scale
    w_o_dil = jax.random.normal(ks[4], (N_DIL_LAYERS, dil_w, D_MODEL), f32) * (dil_w ** -0.5) * DEEPNORM_BETA
    ln_mix_g = 1.0 + 0.02 * jax.random.normal(ks[5], (DEPTH, D_MODEL), f32)
    ln_mix_b = 0.02 * jax.random.normal(ks[6], (DEPTH, D_MODEL), f32)
    w_gate_up = jax.random.normal(ks[7], (DEPTH, D_MODEL, 2 * D_FF), f32) * (D_MODEL ** -0.5)
    w_down = jax.random.normal(ks[8], (DEPTH, D_FF, D_MODEL), f32) * (D_FF ** -0.5) * DEEPNORM_BETA
    ln_ffn_g = 1.0 + 0.02 * jax.random.normal(ks[9], (DEPTH, D_MODEL), f32)
    ln_ffn_b = 0.02 * jax.random.normal(ks[10], (DEPTH, D_MODEL), f32)
    return {'x': x, 'w_qkv_sb': w_qkv_sb, 'w_o_sb': w_o_sb, 'w_qkv_dil': w_qkv_dil, 'w_o_dil': w_o_dil,
            'ln_mix_g': ln_mix_g, 'ln_mix_b': ln_mix_b, 'w_gate_up': w_gate_up, 'w_down': w_down,
            'ln_ffn_g': ln_ffn_g, 'ln_ffn_b': ln_ffn_b}

def reference(x, w_qkv_sb, w_o_sb, w_qkv_dil, w_o_dil, ln_mix_g, ln_mix_b, w_gate_up, w_down, ln_ffn_g, ln_ffn_b):
    cos, sin = rope_tables(x.shape[1], HEAD_DIM)
    for i in range(DEPTH):
        j = i // 2
        if i % 2 == 0:
            mixed = stick_breaking_mixer(x, w_qkv_sb[j], w_o_sb[j])
        else:
            mixed = dilated_mixer(x, w_qkv_dil[j], w_o_dil[j], cos, sin)
        x = layer_norm(DEEPNORM_ALPHA * x + mixed, ln_mix_g[i], ln_mix_b[i])
        x = layer_norm(DEEPNORM_ALPHA * x + swiglu(x, w_gate_up[i], w_down[i]), ln_ffn_g[i], ln_ffn_b[i])
    return x


_drawn_inputs = setup_inputs


def setup_inputs(seed=0):
    import zlib

    import numpy as np

    out = dict(_drawn_inputs(seed))
    spreads = {}
    factors = {'w_o_dil': 2.834}
    for name, (base, spread) in spreads.items():
        noise = np.random.default_rng([zlib.crc32(name.encode()), seed]).standard_normal(out[name].shape)
        drawn = base * np.exp(spread * noise) if base else spread * noise
        out[name] = __import__('jax').numpy.asarray(drawn.astype(out[name].dtype))
    for name, factor in factors.items():
        out[name] = (out[name] * factor).astype(out[name].dtype)
    return out
```

```python
import math
from contextlib import ExitStack

import numpy as np
import concourse.bass as bass
from concourse import mybir

F32 = mybir.dt.float32
F32R = mybir.dt.float32r
ALU = mybir.AluOpType
ACT = mybir.ActivationFunctionType
AX = mybir.AxisListType

P = 128
SEQ = 256
TT = SEQ // P
D = 2048
KT = D // P
HD = 128
SB_HEADS = D // HD
DIL = ((128, 1), (512, 4), (2048, 16))
G = len(DIL)
HPG = 6
DIL_HEADS = G * HPG
FF = -(-(8 * D) // (3 * 256)) * 256
FKT = FF // P
DEPTH = 2
ALPHA = (2.0 * DEPTH) ** 0.25
EPS = 1e-5
SCALE = 1.0 / math.sqrt(HD)
THETA = 10000.0
COLS = 512
GH = COLS // HD
GROUPS = SB_HEADS // GH
PAIRS = FF // COLS
OUTC = D // COLS
NEG = -1e30
SLOTS = 4


class Phase:

    def __init__(self, prev, bodies, cpb, nk, units_per_load, ncols, inc=16, slots=None):
        self.prev, self.bodies, self.cpb, self.nk, self.ncols, self.inc = prev, bodies, cpb, nk, ncols, inc
        self.n = len(nk)
        self.nb = self.n * cpb
        self.k0 = [sum(nk[:u]) for u in range(self.n)]
        self.slot = slots or [u % SLOTS for u in range(self.n)]
        self.load = []
        for l, c in enumerate(units_per_load):
            self.load += [l] * c
        self.loads = len(units_per_load)
        self.first_of = [self.load.index(l) for l in range(self.loads)]
        self.end_of = [self.first_of[l] + units_per_load[l] for l in range(self.loads)]
        self.fills = [sum(l % SLOTS == s for l in range(self.loads)) for s in range(SLOTS)]
        self.u0 = prev.u0 + prev.bodies * prev.nb if prev else 0
        self.c0 = prev.c0 + prev.bodies * prev.cpb if prev else 0
        self.f0 = [prev.f0[s] + prev.fills[s] * prev.inc * prev.bodies * prev.cpb if prev else 0 for s in range(SLOTS)]

    def unit(self, body, ub):
        return body * self.nb + self.u0 + ub

    def chunk(self, body, ub):
        return body * self.cpb + self.c0 + ub // self.n

    def filled(self, body, ub):
        l = self.load[ub % self.n]
        s = l % SLOTS
        c = body * self.cpb + ub // self.n
        return c * (self.fills[s] * self.inc) + self.f0[s] + (l // SLOTS + 1) * self.inc

    def ring_before(self, body, ub, first):
        u, start = ub % self.n, self.unit(body, ub - ub % self.n)
        mine = [v for v in range(u) if self.slot[v] == self.slot[u]]
        if mine:
            return start + mine[-1] + 1
        before = self.prev if first and ub < self.n else self
        if before is None:
            return None
        last = [v for v in range(before.n) if before.slot[v] == self.slot[u]][-1]
        return start - before.n + last + 1

    def raw_before(self, body, cb, l, first):
        start = self.unit(body, cb * self.n)
        if l >= SLOTS:
            return start + self.end_of[l - SLOTS]
        before = self.prev if first and cb == 0 else self
        if before is None:
            return None
        last = [m for m in range(before.loads) if m % SLOTS == l % SLOTS][-1]
        return start - before.n + before.end_of[last]


TWO8 = [2] * 8
PA = Phase(None, GROUPS, 3, TWO8, [2] * 4, COLS)
PB = Phase(PA, OUTC, 1, TWO8, [2] * 4, COLS)
PC = Phase(PB, PAIRS, 2, TWO8, [2] * 4, COLS)
DOWN_SLOTS = [u % SLOTS for u in range(FKT // 2 - 2)] + [2, 3]
PD = Phase(PC, OUTC, 1, [2] * (FKT // 2), [2] * (FKT // 4), COLS, slots=DOWN_SLOTS)
PE_ = Phase(PD, HPG, 3, TWO8, [2] * 4, G * HD, inc=16 * G)
PF = Phase(PE_, OUTC, 1, [2, 1] * HPG, [2] * HPG, COLS)
PG = Phase(PF, PAIRS, 2, TWO8, [2] * 4, COLS)
PH = Phase(PG, OUTC, 1, [2] * (FKT // 2), [2] * (FKT // 4), COLS, slots=DOWN_SLOTS)


def pos_wait(pos):
    return pos["hi"]


def build(nc, x, w_qkv_sb, w_o_sb, w_qkv_dil, w_o_dil, ln_mix_g, ln_mix_b, w_gate_up, w_down, ln_ffn_g, ln_ffn_b,
          tri, rope, masks, out):
    ctx = ExitStack()
    with ctx:
        def sb(name, shape, dt=F32):
            return ctx.enter_context(nc.sbuf_tensor(name, shape, dt))

        def sem(name):
            return ctx.enter_context(nc.semaphore(name))

        resid = sb("resid", [P, TT, D])
        xt_at = (nc.sbuf_base + 31) // 32 * 32
        xt_hi = sb("xt_hi", [P, KT, SEQ], F32R)
        xt_lo = sb("xt_lo", [P, KT, SEQ], F32R)
        raw = sb("raw", [P, SLOTS, 4 * COLS])
        w_hi = sb("w_hi", [P, SLOTS, 2 * COLS], F32R)
        w_lo = sb("w_lo", [P, SLOTS, 2 * COLS], F32R)
        stg = sb("stg", [P, TT, COLS])
        consts = sb("consts", [P, 3, P])
        gbT = sb("gbT", [P, P])
        stats = sb("stats", [P, TT, OUTC, 6])
        mv = sb("mv", [P, TT, 2])
        veps = sb("veps", [P, TT])
        half = sb("half", [P, TT])
        rstd = sb("rstd", [P, TT])
        mx = sb("mx", [P, TT])
        den = sb("den", [P, TT])
        rden = sb("rden", [P, TT])
        arena_bytes = FKT * SEQ * 4
        arena = (nc.sbuf_base + 31) // 32 * 32
        assert arena + 2 * arena_bytes <= nc.sbuf_usable_end

        def placed(name, shape, dt, at):
            return nc.alloc_sbuf_tensor_at(name, shape, dt, offset=at)

        arena_hi = placed("arena_hi", [P, FKT, SEQ], F32R, arena)
        arena_lo = placed("arena_lo", [P, FKT, SEQ], F32R, arena + arena_bytes)
        ident, negtri, negones = consts[:, 0, :], consts[:, 1, :], consts[:, 2, :]
        ot_hi = arena_hi[:, 0:DIL_HEADS, :]
        ot_lo = arena_lo[:, 0:DIL_HEADS, :]
        ot_bytes = DIL_HEADS * SEQ * 4
        n_rest = (FKT - DIL_HEADS) * SEQ
        n_more = n_rest - 2 * D
        rest = placed("mixer_bufs", [P, n_rest], F32, arena + ot_bytes)
        more = placed("mixer_bufs2", [P, n_more], F32, arena + arena_bytes + ot_bytes)
        gb_flat = placed("gb_everywhere", [P, 2 * D], F32, arena + 2 * arena_bytes - 8 * D)
        gb_last = placed("gb_last", [P, 2 * D], F32, xt_at)

        def carve(region, at, *shape):
            n = math.prod(shape)
            v = region[:, at:at + n]
            if len(shape) == 2:
                v = v.rearrange("p (a b) -> p a b", a=shape[0])
            if len(shape) == 3:
                v = v.rearrange("p (a b c) -> p a b c", a=shape[0], b=shape[1])
            return v, at + n

        sq, at = carve(rest, 0, TT, COLS)
        sk, at = carve(rest, at, TT, COLS)
        sv, at = carve(rest, at, TT, COLS)
        qT, at = carve(rest, at, GH, SEQ)
        kT, at = carve(rest, at, GH, SEQ)
        TRI = SEQ + P
        e_buf, at = carve(rest, at, 2, TRI)
        gb_rows, at = carve(rest, at, P)
        assert at <= n_rest
        s_buf, at = carve(more, 0, 2, TRI)
        w_buf, at = carve(more, at, 2, TRI)
        assert at <= n_more
        GC = G * HD
        dq, at = carve(rest, 0, TT, GC)
        dk, at = carve(rest, at, TT, GC)
        dv, at = carve(rest, at, TT, GC)
        dqT, at = carve(rest, at, G, SEQ)
        dkT, at = carve(rest, at, G, SEQ)
        SC = G * P + G * SEQ
        sm, at = carve(rest, at, SC)
        cs_tab, at = carve(rest, at, TT, 2, HD)
        pT, at = carve(rest, at, G, TRI)
        assert at <= n_rest
        mask_sb, at = carve(more, 0, SC)
        rope_a, at = carve(more, at, TT, GC)
        assert at <= n_more
        rope_b = stg[:, :, 0:GC]

        bank = [ctx.enter_context(nc.psum_tensor(f"bank{i}", [P, COLS], F32)) for i in range(8)]
        MAIN, UP, TRB, YB = bank[0:2], bank[2:4], bank[4:6], bank[6:8]
        Z = UP

        consts_in = sem("consts_in")
        x_in = [sem(f"x_in{q}") for q in range(OUTC)]
        rows_in = sem("rows_in")
        gb_in = sem("gb_in")
        tables_in = sem("tables_in")
        gbT_made = sem("gbT_made")
        gbT_ready = sem("gbT_ready")
        half_set = sem("half_set")
        raw_full = [sem(f"raw_full{s}") for s in range(SLOTS)]
        hi_done = sem("hi_done")
        lo_done = sem("lo_done")
        unit_used = sem("unit_used")
        tt0_done = sem("tt0_done")
        xt_turned = sem("xt_turned")
        xt_read = sem("xt_read")
        xt_hi_done = sem("xt_hi_done")
        xt_lo_done = sem("xt_lo_done")
        y_added = sem("y_added")
        y_stats = sem("y_stats")
        ln_mean = sem("ln_mean")
        ln_veps = sem("ln_veps")
        ln_rstd = sem("ln_rstd")
        normed = sem("normed")
        scaled = sem("scaled")
        resid_done = sem("resid_done")
        out_scaled = sem("out_scaled")
        out_scaled_pool = sem("out_scaled_pool")
        out_ready = sem("out_ready")
        out_ready_pool = sem("out_ready_pool")
        out_sent = sem("out_sent")
        sb_free = [sem("sb_free0"), sem("sb_free1")]
        turned = sem("turned")
        turned_act = sem("turned_act")
        turned_dve = sem("turned_dve")
        z_done = sem("z_done")
        abs_done = sem("abs_done")
        exp_done = sem("exp_done")
        log_done = sem("log_done")
        stay_done = sem("stay_done")
        stay_masked = sem("stay_masked")
        later_done = sem("later_done")
        w_done = sem("w_done")
        w_masked = sem("w_masked")
        o_done = sem("o_done")
        o_hi_done = sem("o_hi_done")
        o_free = sem("o_free")
        d_free = [sem("d_free0"), sem("d_free1")]
        rope_parts = sem("rope_parts")
        roped = sem("roped")
        d_turned = sem("d_turned")
        d_turned_act = sem("d_turned_act")
        d_turned_dve = sem("d_turned_dve")
        scores_done = sem("scores_done")
        scores_masked = sem("scores_masked")
        max_done = sem("max_done")
        p_done = sem("p_done")
        rden_done = sem("rden_done")
        p_scaled = sem("p_scaled")
        p_turned = sem("p_turned")
        pT_act = sem("pT_act")
        pT_dve = sem("pT_dve")
        do_done = sem("do_done")
        do_hi_done = sem("do_hi_done")
        do_lo_done = sem("do_lo_done")
        silu_done = [sem(f"silu_done{l}") for l in range(DEPTH)]
        h_done = [sem(f"h_done{l}") for l in range(DEPTH)]
        h_turned = [sem(f"h_turned{l}") for l in range(DEPTH)]
        ht_hi_done = [sem(f"ht_hi_done{l}") for l in range(DEPTH)]
        ht_lo_done = [sem(f"ht_lo_done{l}") for l in range(DEPTH)]

        IN_BODY = dict(score=1, mask=3, top=4, exp=5, norm=6, turn=9, take=11, turn2=12, take2=14, pv=15, hi=17, lo=18)
        AT_END = dict(score=1, mask=3, top=3, exp=4, norm=5, turn=6, take=7, turn2=8, take2=9, pv=9, hi=10, lo=10)

        rows_k = "(k p) n -> p k n"

        def gb_col(ln, which, kt):
            return (ln % 2) * 64 + which * 32 + (ln // 2) * KT + kt

        def gb_rows_of(ln):
            gain, bias = (ln_mix_g, ln_mix_b) if ln % 2 == 0 else (ln_ffn_g, ln_ffn_b)
            return gain[ln // 2:ln // 2 + 1, :], bias[ln // 2:ln // 2 + 1, :]

        block = ctx.enter_context(nc.Block())

        @block.sync
        def _(sp):
            def load(ph, body, cb, l, first, source):
                before = ph.raw_before(body, cb, l, first)
                if before is not None:
                    sp.wait_ge(lo_done, before)
                u = ph.first_of[l]
                k0, nk = ph.k0[u], sum(ph.nk[u:ph.end_of[l]])
                dst = raw[:, l % SLOTS, 0:nk * ph.ncols].rearrange("p (k n) -> p k n", k=nk)
                for d, s in source(body, cb, l, k0, nk, dst):
                    sp.dma_start(d, s).then_inc(raw_full[l % SLOTS], 16)

            def walk(ph, source):
                for cb in range(ph.cpb):
                    for l in range(ph.loads):
                        load(ph, 0, cb, l, True, source)
                with sp.Fori(1, ph.bodies) as i:
                    for cb in range(ph.cpb):
                        for l in range(ph.loads):
                            load(ph, i, cb, l, False, source)

            def plain(w, col):
                def source(body, cb, l, k0, nk, dst):
                    rows = w[k0 * P:(k0 + nk) * P, bass.ds(col(body, cb), COLS)]
                    return [(dst, rows.rearrange(rows_k, p=P))]
                return source

            def dilated_qkv(body, cb, l, k0, nk, dst):
                for g in range(G):
                    col = body * HD + (cb * DIL_HEADS + g * HPG) * HD
                    rows = w_qkv_dil[0, k0 * P:(k0 + nk) * P, bass.ds(col, HD)]
                    yield dst[:, :, g * HD:(g + 1) * HD], rows.rearrange(rows_k, p=P)

            def dilated_out(body, cb, l, k0, nk, dst):
                by_head = w_o_dil[0].rearrange("(g h p) n -> h p g n", g=G, h=HPG)
                return [(dst, by_head[l, :, :, bass.ds(body * COLS, COLS)])]

            sp.dma_start(consts[:, :, :], tri).then_inc(consts_in, 16)
            for q in range(OUTC):
                sp.dma_start(resid[:, :, q * COLS:(q + 1) * COLS],
                             x[0, :, q * COLS:(q + 1) * COLS].rearrange("(t p) d -> p t d", p=P)).then_inc(x_in[q], 16)
                load(PA, 0, 0, q, True, plain(w_qkv_sb[0], lambda body, cb: 0))
            for v, rows in enumerate((ln_mix_g, ln_mix_b, ln_ffn_g, ln_ffn_b)):
                sp.dma_start(gb_rows[v * 2 * KT:(v + 1) * 2 * KT, :],
                             rows.rearrange("l (k p) -> (l k) p", p=P)).then_inc(rows_in, 16)
            qkv_sb = plain(w_qkv_sb[0], lambda body, cb: body * COLS + cb * D)
            for cb in range(1, PA.cpb):
                for l in range(PA.loads):
                    load(PA, 0, cb, l, True, qkv_sb)
            with sp.Fori(1, PA.bodies) as i:
                for cb in range(PA.cpb):
                    for l in range(PA.loads):
                        load(PA, i, cb, l, False, qkv_sb)
            walk(PB, plain(w_o_sb[0], lambda body, cb: body * COLS))
            walk(PC, plain(w_gate_up[0], lambda body, cb: body * COLS + cb * FF))
            walk(PD, plain(w_down[0], lambda body, cb: body * COLS))
            walk(PE_, dilated_qkv)
            walk(PF, dilated_out)
            walk(PG, plain(w_gate_up[1], lambda body, cb: body * COLS + cb * FF))
            walk(PH, plain(w_down[1], lambda body, cb: body * COLS))
            for q in range(OUTC):
                if q == 0:
                    sp.wait_ge(out_ready_pool, TT)
                else:
                    sp.wait_ge(out_ready, TT * q)
                sp.dma_start(out[0, :, q * COLS:(q + 1) * COLS].rearrange("(t p) d -> p t d", p=P),
                             resid[:, :, q * COLS:(q + 1) * COLS]).then_inc(out_sent, 16)
            sp.wait_ge(out_sent, 16 * OUTC)

        @block.tensor
        def _(pe):
            def unit(ph, body, ub, a_hi, a_lo, banks, free=None):
                u, w = ub % ph.n, ph.ncols
                pe.wait_ge(lo_done, ph.unit(body, ub) + 1)
                for tt in range(TT):
                    if free is not None:
                        pe.wait_ge(*free[tt])
                    for kk in range(ph.nk[u]):
                        col = slice(kk * w, (kk + 1) * w)
                        terms = ((a_hi, w_hi), (a_hi, w_lo), (a_lo, w_hi))
                        for n, (a, b) in enumerate(terms):
                            mm = nc.tensor.matmul(banks[tt][:, 0:w], a[:, ph.k0[u] + kk, tt * P:(tt + 1) * P],
                                                  b[:, ph.slot[u], col], start=(u == 0 and kk == 0 and n == 0),
                                                  stop=(u == ph.n - 1 and kk == ph.nk[u] - 1 and n == 2))
                    if tt == 0 and u == ph.n - 1:
                        mm.then_inc(tt0_done, 1)
                mm.then_inc(unit_used, 1)

            def turn_x(ev, r):
                if ev == 0:
                    pe.wait_ge(x_in[r // 2], 16)
                else:
                    pe.wait_ge(normed, 8 * (ev - 1) + 2 * (r // 2) + 2)
                if r >= 2:
                    pe.wait_ge(xt_read, 8 * ev + r - 1)
                for kk in range(2):
                    for tt in range(TT):
                        k = 2 * r + kk
                        t = nc.tensor.transpose(TRB[r % 2][:, (2 * kk + tt) * P:(2 * kk + tt + 1) * P],
                                                resid[:, tt, k * P:(k + 1) * P], ident)
                t.then_inc(xt_turned, 1)

            def x_before(ev, ub):
                if ub == 0:
                    turn_x(ev, 0)
                if ub < KT // 2 - 1:
                    turn_x(ev, ub + 1)
                if ub < KT // 2:
                    pe.wait_ge(xt_lo_done, 8 * ev + ub + 1)

            def sb_scores(g, h):
                pe.wait_ge((turned_act, turned_dve)[h // 2], g * 2 + 2)
                nc.tensor.matmul(Z[h % 2][:, 0:SEQ], kT[:, h, 0:P], qT[:, h, :], start=True, stop=True,
                                 skip_group_check=True)
                nc.tensor.matmul(Z[h % 2][:, SEQ:TRI], kT[:, h, P:SEQ], qT[:, h, P:SEQ], start=False, stop=True,
                                 skip_group_check=True).then_inc(z_done, 1)

            def sb_later(g, h):
                pe.wait_ge(stay_masked, g * GH + h + 1)
                nc.tensor.matmul(Z[h % 2][:, 0:TRI], negtri, s_buf[:, h % 2, :], start=False, stop=True,
                                 skip_group_check=True)
                nc.tensor.matmul(Z[h % 2][:, P:SEQ], negones, s_buf[:, h % 2, SEQ:TRI], start=False, stop=True,
                                 skip_group_check=True).then_inc(later_done, 1)

            def sb_values(g, h, banks):
                pe.wait_ge(w_masked, g * GH + h + 1)
                pe.wait_ge(sb_free[0], g * 3 + 3)
                pe.wait_ge(sb_free[1], g * 3 + 3)
                pe.wait_ge(o_free, g * GH + h + 1)
                cols = slice(h * HD, (h + 1) * HD)
                nc.tensor.matmul(banks[h % 2][:, 0:SEQ], sv[:, 0, cols], w_buf[:, h % 2, 0:SEQ], start=True, stop=False,
                                 skip_group_check=True)
                nc.tensor.matmul(banks[h % 2][:, P:SEQ], sv[:, 1, cols], w_buf[:, h % 2, SEQ:TRI], start=False,
                                 stop=True, skip_group_check=True).then_inc(o_done, 1)

            def sb_turn(i, part, src):
                for tt in range(TT):
                    pe.wait_ge(sb_free[tt], i * 3 + part + 1)
                if part == 1:
                    pe.wait_ge(turned_act, i * 2 + 1)
                    pe.wait_ge(turned_dve, i * 2 + 1)
                for h in range(GH):
                    for tt in range(TT):
                        at = (h % 2) * SEQ + tt * P
                        t = nc.tensor.transpose(TRB[h // 2][:, at:at + P], src[:, tt, h * HD:(h + 1) * HD], ident)
                    if h % 2:
                        t.then_inc(turned, 1)

            def sb_body(i, first):
                for ub in range(PA.nb):
                    part = ub // PA.n
                    if first and part == 0:
                        x_before(0, ub)
                    free = None
                    if ub % PA.n == 0 and not (first and part == 0):
                        free = [(sb_free[tt], i * 3 + part) for tt in range(TT)]
                    unit(PA, i, ub, xt_hi, xt_lo, MAIN, free)
                    if first and ub == 9:
                        pe.wait_ge(rows_in, 64)
                        nc.tensor.transpose(YB[1][:, 0:P], gb_rows[:, :], ident).then_inc(gbT_made, 1)
                    if not first:
                        h, step = divmod(ub - 1, 4)
                        if ub >= 1 and step == 0 and h < GH:
                            sb_scores(i - 1, h)
                        h, step = divmod(ub - 4, 4)
                        if ub >= 4 and step == 0 and h < GH:
                            sb_later(i - 1, h)
                        h, step = divmod(ub - 7, 4)
                        if ub >= 7 and step == 0 and h < GH:
                            sb_values(i - 1, h, YB)
                    if ub == 17:
                        sb_turn(i, 0, sq)
                    if ub == 20:
                        sb_turn(i, 1, sk)

            pe.wait_ge(consts_in, 16)
            sb_body(0, True)
            with pe.Fori(1, GROUPS) as i:
                sb_body(i, False)

            def y_chunk(ph, ln, c, a_hi, a_lo, first, ub):
                free = None
                if ub == 0 and not first:
                    free = [(y_added, c * 2 + (8 * ln - 1 + tt)) for tt in range(TT)]
                unit(ph, c, ub, a_hi, a_lo, YB, free)

            def y_rest(ph, ln, a_hi, a_lo):
                with pe.Fori(1, OUTC) as c:
                    for ub in range(ph.nb):
                        y_chunk(ph, ln, c, a_hi, a_lo, False, ub)

            last = GROUPS - 1
            pe.wait_ge(o_free, GH * last + 2)
            for ub in range(PB.nb):
                if ub == 6:
                    pe.wait_ge(o_free, GH * last + 2 + 2)
                if ub == 7:
                    for h in (2, 3):
                        sb_values(last, h, MAIN)
                    pe.wait_ge(o_free, GH * last + 4 + 2)
                y_chunk(PB, 0, 0, ot_hi, ot_lo, True, ub)
                if ub == 0:
                    sb_scores(last, 0)
                    sb_scores(last, 1)
                if ub == 2:
                    sb_later(last, 0)
                    sb_later(last, 1)
                if ub == 3:
                    for h in (2, 3):
                        pe.wait_ge(w_done, GH * last + h - 1)
                        sb_scores(last, h)
                if ub == 4:
                    sb_values(last, 0, MAIN)
                    sb_values(last, 1, MAIN)
                if ub == 5:
                    sb_later(last, 2)
                    sb_later(last, 3)
            y_rest(PB, 0, ot_hi, ot_lo)

            def turn_h(l, c):
                pe.wait_ge(h_done[l], c * 2 + 2)
                pe.wait_ge(ht_lo_done[l], c * 2)
                for r in range(2):
                    for kk in range(2):
                        for tt in range(TT):
                            k = 2 * r + kk
                            t = nc.tensor.transpose(TRB[r][:, (2 * kk + tt) * P:(2 * kk + tt + 1) * P],
                                                    stg[:, tt, k * P:(k + 1) * P], ident)
                    t.then_inc(h_turned[l], 1)

            def pair(ph, l, ev, c, first):
                for ub in range(ph.nb):
                    if first:
                        x_before(ev, ub)
                    banks = (MAIN, UP)[ub // ph.n]
                    free = None
                    if ub % ph.n == 0 and not first:
                        read = (silu_done, h_done)[ub // ph.n][l]
                        free = [(read, c * 2 - 1 + tt) for tt in range(TT)]
                    unit(ph, c, ub, xt_hi, xt_lo, banks, free)
                    if ub == 4 and not first:
                        turn_h(l, c - 1)

            def swiglu(pg, pd, l):
                ev = 2 * l + 1
                pair(pg, l, ev, 0, True)
                with pe.Fori(1, PAIRS) as c:
                    pair(pg, l, ev, c, False)
                for ub in range(pd.nb):
                    if ub == 0:
                        pe.wait_ge(ht_lo_done[l], 2 * (PAIRS - 1))
                    if ub >= pd.nb - 2:
                        pe.wait_ge(ht_lo_done[l], 2 * (PAIRS - 1) + ub - (pd.nb - 2) + 1)
                    y_chunk(pd, 2 * l + 1, 0, arena_hi, arena_lo, True, ub)
                    if ub == 4:
                        turn_h(l, PAIRS - 1)
                y_rest(pd, 2 * l + 1, arena_hi, arena_lo)

            swiglu(PC, PD, 0)

            def d_turn(i, part, src):
                pe.wait_ge(roped, i * 4 + 2 * part + 2)
                if part == 1:
                    pe.wait_ge(d_turned_act, i * 2 + 1)
                    pe.wait_ge(d_turned_dve, i * 2 + 1)
                for g in range(G):
                    for tt in range(TT):
                        at = (g % 2) * SEQ + tt * P
                        t = nc.tensor.transpose(TRB[g // 2][:, at:at + P], src[:, tt, g * HD:(g + 1) * HD], ident)
                    if g >= 1:
                        t.then_inc(d_turned, 1)

            def d_steps(ub, h, pos, second, third):
                if ub == pos["score"]:
                    pe.wait_ge(d_turned_act, h * 2 + 2)
                    pe.wait_ge(d_turned_dve, h * 2 + 2)
                    pe.wait_ge(do_lo_done, h * 2)
                    for g in range(G):
                        nc.tensor.matmul(Z[0][:, g * P:(g + 1) * P], dqT[:, g, 0:P], dkT[:, g, 0:P], start=True,
                                         stop=True)
                    for g in range(2):
                        nc.tensor.matmul(Z[1][:, g * SEQ:(g + 1) * SEQ], dqT[:, g, P:SEQ], dkT[:, g, :], start=True,
                                         stop=True)
                    nc.tensor.matmul(third[:, 0:SEQ], dqT[:, 2, P:SEQ], dkT[:, 2, :], start=True,
                                     stop=True).then_inc(scores_done, 1)
                if ub == pos["turn"]:
                    pe.wait_ge(p_scaled, h * 2 + 2)
                for g in range(G):
                    if ub == pos["turn2" if g == 2 else "turn"]:
                        if g == 2:
                            pe.wait_ge(pT_act, h * 2 + 1)
                        for n, at in enumerate((g * P, G * P + g * SEQ, G * P + g * SEQ + P)):
                            t = nc.tensor.transpose(TRB[g % 2][:, n * P:(n + 1) * P], sm[:, at:at + P], ident)
                        t.then_inc(p_turned, 1)
                if ub == pos["pv"]:
                    pe.wait_ge(pT_act, h * 2 + 2)
                    pe.wait_ge(pT_dve, h + 1)
                    for tt in range(TT):
                        pe.wait_ge(d_free[tt], h * 3 + 3)
                    for g in range(G):
                        dst, at = (second, g * SEQ) if g < 2 else (third, 0)
                        cols = slice(g * HD, (g + 1) * HD)
                        nc.tensor.matmul(dst[:, at:at + SEQ], dv[:, 0, cols], pT[:, g, 0:SEQ], start=True, stop=False,
                                         skip_group_check=True)
                        t = nc.tensor.matmul(dst[:, at + P:at + SEQ], dv[:, 1, cols], pT[:, g, SEQ:TRI], start=False,
                                             stop=True, skip_group_check=True)
                        if g >= 1:
                            t.then_inc(do_done, 1)

            def d_body(i, first):
                for ub in range(PE_.nb):
                    part = ub // PE_.n
                    if first and part == 0:
                        x_before(2, ub)
                    free = None
                    if ub % PE_.n == 0 and not (first and part == 0):
                        free = [(d_free[tt], i * 3 + part) for tt in range(TT)]
                    unit(PE_, i, ub, xt_hi, xt_lo, MAIN, free)
                    if not first:
                        d_steps(ub, i - 1, IN_BODY, YB[1], YB[0])
                    if ub == 17:
                        d_turn(i, 0, dq)
                    if ub == 21:
                        d_turn(i, 1, dk)

            d_body(0, True)
            with pe.Fori(1, HPG) as i:
                d_body(i, False)
            pe.wait_ge(do_lo_done, 2 * (HPG - 1))
            for ub in range(PF.nb):
                if ub == pos_wait(AT_END):
                    pe.wait_ge(do_lo_done, 2 * HPG)
                y_chunk(PF, 2, 0, ot_hi, ot_lo, True, ub)
                if ub == AT_END["score"]:
                    for tt in range(TT):
                        pe.wait_ge(d_free[tt], 3 * HPG)
                d_steps(ub, HPG - 1, AT_END, MAIN[0], MAIN[1])
            y_rest(PF, 2, ot_hi, ot_lo)

            swiglu(PG, PH, 1)

        @block.scalar
        def _(act):
            def split(ph, body, ub, first):
                u = ub % ph.n
                l = ph.load[u]
                if u == ph.first_of[l]:
                    act.wait_ge(raw_full[l % SLOTS], ph.filled(body, ub))
                before = ph.ring_before(body, ub, first)
                if before is not None:
                    act.wait_ge(unit_used, before)
                at, n = (ph.k0[u] - ph.k0[ph.first_of[l]]) * ph.ncols, ph.nk[u] * ph.ncols
                nc.scalar.activation(w_hi[:, ph.slot[u], 0:n], raw[:, l % SLOTS, at:at + n], ACT.Copy).then_inc(hi_done, 1)

            def x_round(ev, r):
                act.wait_ge(xt_turned, 8 * ev + r + 1)
                if r >= 2:
                    act.wait_ge(xt_lo_done, 8 * ev + r - 1)
                tmp = stg[:, r % 2, :]
                if ev == 0:
                    nc.scalar.activation(tmp, TRB[r % 2][:, :], ACT.Copy).then_inc(xt_read, 1)
                else:
                    for kk in range(2):
                        g, b = (gb_col(ev - 1, v, 2 * r + kk) for v in range(2))
                        a = nc.scalar.activation(tmp[:, kk * SEQ:(kk + 1) * SEQ], TRB[r % 2][:, kk * SEQ:(kk + 1) * SEQ],
                                                 ACT.Identity, bias=gbT[:, b:b + 1], scale=gbT[:, g:g + 1])
                    a.then_inc(xt_read, 1)
                act.wait_ge(xt_read, 8 * ev + r + 1)
                nc.scalar.activation(xt_hi[:, 2 * r:2 * r + 2, :], tmp.rearrange("p (k n) -> p k n", k=2),
                                     ACT.Copy).then_inc(xt_hi_done, 1)

            def x_before(ev, ub):
                if 3 <= ub < 3 + KT // 2:
                    x_round(ev, ub - 3)

            def stage(tt0_chunk, dst, width, free):
                act.wait_ge(tt0_done, tt0_chunk + 1)
                nc.scalar.activation(dst[:, 0, :], MAIN[0][:, 0:width], ACT.Copy).then_inc(free[0], 1)

            def sb_log(g, h):
                e = e_buf[:, h % 2, :]
                act.wait_ge(z_done, g * GH + h + 1)
                nc.scalar.activation(e, Z[h % 2][:, 0:TRI], ACT.Abs).then_inc(abs_done, 1)
                act.wait_ge(abs_done, g * GH + h + 1)
                nc.scalar.activation(e, e, ACT.Exp, scale=-1.0).then_inc(exp_done, 1)
                act.wait_ge(exp_done, g * GH + h + 1)
                nc.scalar.activation(e, e, ACT.Ln, bias=1.0).then_inc(log_done, 1)

            def sb_weights(g, h):
                act.wait_ge(later_done, g * GH + h + 1)
                nc.scalar.activation(w_buf[:, h % 2, :], Z[h % 2][:, 0:TRI], ACT.Exp).then_inc(w_done, 1)

            def sb_out(g, h, banks):
                act.wait_ge(o_done, g * GH + h + 1)
                head = bass.ds(g * GH + h, 1)
                nc.scalar.activation(ot_hi[:, head, :].rearrange("p a n -> p (a n)"), banks[h % 2][:, 0:SEQ],
                                     ACT.Copy).then_inc(o_hi_done, 1)

            def sb_body(i, first):
                for ub in range(PA.nb):
                    if first:
                        x_before(0, ub)
                    split(PA, i, ub, first)
                    if first and ub == 12:
                        act.wait_ge(gbT_made, 1)
                        nc.scalar.activation(gbT[:, :], YB[1][:, 0:P], ACT.Copy).then_inc(gbT_ready, 1)
                    if not first:
                        if ub == 1:
                            stage(i * 3 + (PA.c0 - 1), sv, COLS, sb_free)
                        h, step = divmod(ub - 3, 4)
                        if ub >= 3 and step == 0 and h < GH:
                            sb_log(i - 1, h)
                        h, step = divmod(ub - 6, 4)
                        if ub >= 6 and step == 0 and h < GH:
                            sb_weights(i - 1, h)
                        h, step = divmod(ub - 9, 4)
                        if ub >= 9 and step == 0 and h < GH:
                            sb_out(i - 1, h, YB)
                    if ub == (10 if first else 9):
                        stage(i * 3 + PA.c0, sq, COLS, sb_free)
                    if ub == 17:
                        stage(i * 3 + (PA.c0 + 1), sk, COLS, sb_free)
                    if ub == 19:
                        act.wait_ge(turned, i * 4 + 1)
                        nc.scalar.activation(qT[:, 0:2, :], TRB[0][:, :].rearrange("p (h n) -> p h n", h=2), ACT.Copy,
                                             scale=SCALE).then_inc(turned_act, 1)
                    if ub == 22:
                        act.wait_ge(turned, i * 4 + 3)
                        nc.scalar.activation(kT[:, 0:2, :], TRB[0][:, :].rearrange("p (h n) -> p h n", h=2),
                                             ACT.Copy).then_inc(turned_act, 1)

            sb_body(0, True)
            with act.Fori(1, GROUPS) as i:
                sb_body(i, False)

            def rest(ph):
                with act.Fori(1, ph.bodies) as c:
                    for ub in range(ph.nb):
                        split(ph, c, ub, False)

            last = GROUPS - 1
            for ub in range(PB.nb):
                split(PB, 0, ub, True)
                if ub == 1:
                    stage(PB.c0 - 1, sv, COLS, sb_free)
                    sb_log(last, 0)
                    sb_log(last, 1)
                if ub == 3:
                    sb_weights(last, 0)
                    sb_weights(last, 1)
                if ub == 5:
                    sb_log(last, 2)
                    sb_log(last, 3)
                if ub == 6:
                    sb_out(last, 0, MAIN)
                    sb_out(last, 1, MAIN)
                if ub == 7:
                    sb_weights(last, 2)
                    sb_weights(last, 3)
                    sb_out(last, 2, MAIN)
                    sb_out(last, 3, MAIN)
            rest(PB)

            def ht_hi(l, c):
                for r in range(2):
                    act.wait_ge(h_turned[l], c * 2 + r + 1)
                    nc.scalar.activation(arena_hi[:, bass.ds(c * 4 + 2 * r, 2), :],
                                         TRB[r][:, :].rearrange("p (k n) -> p k n", k=2),
                                         ACT.Copy).then_inc(ht_hi_done[l], 1)

            def pair(ph, l, ev, c, first):
                for ub in range(ph.nb):
                    if first:
                        x_before(ev, ub)
                    split(ph, c, ub, first)
                    if ub == 7 and not first:
                        ht_hi(l, c - 1)
                    if ub == (10 if first else 9):
                        if first:
                            act.wait_ge(xt_lo_done, 8 * ev + KT // 2)
                        else:
                            act.wait_ge(h_turned[l], c * 2)
                        for tt in range(TT):
                            if tt == 0:
                                act.wait_ge(tt0_done, c * 2 + ph.c0 + 1)
                            else:
                                act.wait_ge(unit_used, ph.unit(c, ph.n))
                            nc.scalar.activation(stg[:, tt, :], MAIN[tt][:, :], ACT.Silu).then_inc(silu_done[l], 1)

            def swiglu(pg, pd, l):
                ev = 2 * l + 1
                pair(pg, l, ev, 0, True)
                with act.Fori(1, PAIRS) as c:
                    pair(pg, l, ev, c, False)
                for ub in range(pd.nb):
                    split(pd, 0, ub, True)
                    if ub == 6:
                        ht_hi(l, PAIRS - 1)
                rest(pd)

            act.wait_ge(gbT_ready, 1)
            swiglu(PC, PD, 0)

            def d_steps(ub, h, pos, second, third):
                if ub == pos["exp"]:
                    for t, cols in ((0, slice(0, G * P)), (1, slice(G * P, SC))):
                        act.wait_ge(max_done, h * 2 + t + 1)
                        nc.scalar.activation(sm[:, cols], sm[:, cols], ACT.Exp, bias=mx[:, t:t + 1],
                                             accum_out=den[:, t:t + 1]).then_inc(p_done, 1)
                for g in (0, 2):
                    if ub == pos["take" if g == 0 else "take2"]:
                        act.wait_ge(p_turned, h * 3 + g + 1)
                        nc.scalar.activation(pT[:, g, :], TRB[0][:, 0:TRI], ACT.Copy).then_inc(pT_act, 1)
                if ub == pos["hi"]:
                    act.wait_ge(do_done, h * 2 + 1)
                    nc.scalar.activation(ot_hi[:, bass.ds(h * G, 2), :],
                                         second[:, :].rearrange("p (k n) -> p k n", k=2), ACT.Copy).then_inc(do_hi_done, 1)
                    act.wait_ge(do_done, h * 2 + 2)
                    nc.scalar.activation(ot_hi[:, bass.ds(h * G + 2, 1), :].rearrange("p a n -> p (a n)"),
                                         third[:, 0:SEQ], ACT.Copy).then_inc(do_hi_done, 1)

            def d_body(i, first):
                for ub in range(PE_.nb):
                    if first:
                        x_before(2, ub)
                    split(PE_, i, ub, first)
                    if not first:
                        if ub == 1:
                            stage(i * 3 + (PE_.c0 - 1), dv, GC, d_free)
                        d_steps(ub, i - 1, IN_BODY, YB[1], YB[0])
                    if ub == 19:
                        act.wait_ge(d_turned, i * 4 + 1)
                        nc.scalar.activation(dqT[:, 0:2, :], TRB[0][:, :].rearrange("p (h n) -> p h n", h=2),
                                             ACT.Copy).then_inc(d_turned_act, 1)
                    if ub == 23:
                        act.wait_ge(d_turned, i * 4 + 3)
                        nc.scalar.activation(dkT[:, 0:2, :], TRB[0][:, :].rearrange("p (h n) -> p h n", h=2),
                                             ACT.Copy).then_inc(d_turned_act, 1)

            d_body(0, True)
            with act.Fori(1, HPG) as i:
                d_body(i, False)
            for ub in range(PF.nb):
                split(PF, 0, ub, True)
                if ub == 1:
                    stage(PF.c0 - 1, dv, GC, d_free)
                d_steps(ub, HPG - 1, AT_END, MAIN[0], MAIN[1])
            rest(PF)

            swiglu(PG, PH, 1)

        @block.vector
        def _(dve):
            def split(ph, body, ub):
                u = ub % ph.n
                l = ph.load[u]
                dve.wait_ge(hi_done, ph.unit(body, ub) + 1)
                at, n = (ph.k0[u] - ph.k0[ph.first_of[l]]) * ph.ncols, ph.nk[u] * ph.ncols
                nc.vector.tensor_tensor(w_lo[:, ph.slot[u], 0:n], raw[:, l % SLOTS, at:at + n],
                                        w_hi[:, ph.slot[u], 0:n].bitcast(F32), ALU.subtract).then_inc(lo_done, 1)

            def norm(ln, q):
                for tt in range(TT):
                    part = resid[:, tt, q * COLS:(q + 1) * COLS]
                    nc.vector.tensor_scalar(part, part, mv[:, tt, 0:1], rstd[:, tt:tt + 1], ALU.subtract,
                                            ALU.mult).then_inc(normed, 1)

            def y_take(ph, ln, c):
                for tt in range(TT):
                    if tt == 0:
                        dve.wait_ge(tt0_done, c + (ph.c0 + 1))
                    else:
                        dve.wait_ge(unit_used, ph.unit(c, ph.n))
                    part = resid[:, tt, bass.ds(c * COLS, COLS)]
                    nc.vector.scalar_tensor_tensor(out=part, in0=part, scalar=ALPHA, in1=YB[tt][:, :], op0=ALU.mult,
                                                   op1=ALU.add).then_inc(y_added, 1)
                for tt in range(TT):
                    dve.wait_ge(y_added, c * 2 + (8 * ln + tt + 1))
                    nc.vector.bn_stats(stats[:, tt, bass.ds(c, 1), :].rearrange("p a s -> p (a s)"),
                                       resid[:, tt, bass.ds(c * COLS, COLS)]).then_inc(y_stats, 1)

            def moments(ln):
                dve.wait_ge(y_stats, 8 * (ln + 1))
                for tt in range(TT):
                    nc.vector.bn_aggr(mv[:, tt, :], stats[:, tt, :, :].rearrange("p c s -> p (c s)")).then_inc(ln_mean, 1)
                dve.wait_ge(ln_mean, 2 * (ln + 1))
                nc.vector.tensor_scalar(veps[:, :], mv[:, :, 1], EPS, None, ALU.add).then_inc(ln_veps, 1)
                dve.wait_ge(ln_rstd, ln + 1)

            def x_before(ev, ub):
                if ub == 2 and ev > 0:
                    moments(ev - 1)
                    norm(ev - 1, 0)
                    norm(ev - 1, 1)
                if 3 <= ub < 3 + KT // 2:
                    r = ub - 3
                    dve.wait_ge(xt_hi_done, 8 * ev + r + 1)
                    nc.vector.tensor_tensor(xt_lo[:, 2 * r:2 * r + 2, :], stg[:, r % 2, :].rearrange("p (k n) -> p k n", k=2),
                                            xt_hi[:, 2 * r:2 * r + 2, :].bitcast(F32), ALU.subtract).then_inc(xt_lo_done, 1)
                    if ev > 0 and r in (0, 2):
                        norm(ev - 1, r // 2 + 2)

            def stage(units, dst, width, free):
                dve.wait_ge(unit_used, units)
                nc.vector.tensor_copy(dst[:, 1, :], MAIN[1][:, 0:width]).then_inc(free[1], 1)

            def sb_stay(g, h):
                dve.wait_ge(log_done, g * GH + h + 1)
                nc.vector.scalar_tensor_tensor(out=s_buf[:, h % 2, :], in0=Z[h % 2][:, 0:TRI], scalar=0.0,
                                               in1=e_buf[:, h % 2, :], op0=ALU.max, op1=ALU.add).then_inc(stay_done, 1)

            def sb_out(g, h, banks):
                dve.wait_ge(o_hi_done, g * GH + h + 1)
                head = bass.ds(g * GH + h, 1)
                nc.vector.tensor_tensor(ot_lo[:, head, :].rearrange("p a n -> p (a n)"), banks[h % 2][:, 0:SEQ],
                                        ot_hi[:, head, :].rearrange("p a n -> p (a n)").bitcast(F32),
                                        ALU.subtract).then_inc(o_free, 1)

            def sb_body(i, first):
                for ub in range(PA.nb):
                    if first:
                        x_before(0, ub)
                    split(PA, i, ub)
                    if not first:
                        if ub == 1:
                            stage(PA.unit(i, 0), sv, COLS, sb_free)
                        h, step = divmod(ub - 4, 4)
                        if ub >= 4 and step == 0 and h < GH:
                            sb_stay(i - 1, h)
                        h, step = divmod(ub - 10, 4)
                        if ub >= 10 and step == 0 and h < GH:
                            sb_out(i - 1, h, YB)
                    if ub == (10 if first else 9):
                        stage(PA.unit(i, PA.n), sq, COLS, sb_free)
                    if ub == 17:
                        stage(PA.unit(i, 2 * PA.n), sk, COLS, sb_free)
                    if ub == 19:
                        dve.wait_ge(turned, i * 4 + 2)
                        nc.vector.tensor_scalar(qT[:, 2:4, :], TRB[1][:, :].rearrange("p (h n) -> p h n", h=2), SCALE, None,
                                                ALU.mult).then_inc(turned_dve, 1)
                    if ub == 22:
                        dve.wait_ge(turned, i * 4 + 4)
                        nc.vector.tensor_copy(kT[:, 2:4, :], TRB[1][:, :].rearrange("p (h n) -> p h n", h=2)).then_inc(
                            turned_dve, 1)

            nc.vector.memset(mx[:, :], 0.0).then_inc(o_free, 2)
            sb_body(0, True)
            with dve.Fori(1, GROUPS) as i:
                sb_body(i, False)

            def y_rest(ph, ln):
                if ln > 0:
                    dve.wait_ge(resid_done, 8 * ln)
                with dve.Fori(1, OUTC) as c:
                    for ub in range(ph.nb):
                        split(ph, c, ub)
                        if ub == 1:
                            y_take(ph, ln, c - 1)

            last = GROUPS - 1
            for ub in range(PB.nb):
                split(PB, 0, ub)
                if ub == 1:
                    stage(PB.u0, sv, COLS, sb_free)
                if ub == 2:
                    sb_stay(last, 0)
                    sb_stay(last, 1)
                if ub == 5:
                    sb_stay(last, 2)
                    sb_stay(last, 3)
                if ub == 6:
                    sb_out(last, 0, MAIN)
                    sb_out(last, 1, MAIN)
                if ub == 7:
                    sb_out(last, 2, MAIN)
                    sb_out(last, 3, MAIN)
            y_rest(PB, 0)

            def h_take(ph, l, c):
                for tt in range(TT):
                    dve.wait_ge(silu_done[l], c * 2 + tt + 1)
                    if tt == 0:
                        dve.wait_ge(tt0_done, c * 2 + ph.c0 + 2)
                    else:
                        dve.wait_ge(unit_used, ph.unit(c, ph.nb))
                    nc.vector.tensor_tensor(stg[:, tt, :], stg[:, tt, :], UP[tt][:, :], ALU.mult).then_inc(h_done[l], 1)

            def ht_lo(l, c):
                for r in range(2):
                    dve.wait_ge(ht_hi_done[l], c * 2 + r + 1)
                    tiles = bass.ds(c * 4 + 2 * r, 2)
                    nc.vector.tensor_tensor(arena_lo[:, tiles, :], TRB[r][:, :].rearrange("p (k n) -> p k n", k=2),
                                            arena_hi[:, tiles, :].bitcast(F32), ALU.subtract).then_inc(ht_lo_done[l], 1)

            def pair(pd_before, ph, l, ev, c, first):
                for ub in range(ph.nb):
                    if first:
                        if ub == 2:
                            y_take(pd_before, ev - 1, OUTC - 1)
                        x_before(ev, ub)
                    split(ph, c, ub)
                    if not first:
                        if ub == 1:
                            h_take(ph, l, c - 1)
                        if ub == 8:
                            ht_lo(l, c - 1)

            def swiglu(before, pg, pd, l):
                ev = 2 * l + 1
                pair(before, pg, l, ev, 0, True)
                dve.wait_ge(resid_done, 8 * ev)
                with dve.Fori(1, PAIRS) as c:
                    pair(before, pg, l, ev, c, False)
                for ub in range(pd.nb):
                    split(pd, 0, ub)
                    if ub == 1:
                        h_take(pg, l, PAIRS - 1)
                    if ub == 7:
                        ht_lo(l, PAIRS - 1)
                y_rest(pd, ev)

            swiglu(PB, PC, PD, 0)

            def rope_half(i, part, tt, dst):
                if tt == 0:
                    dve.wait_ge(tt0_done, i * 3 + (PE_.c0 + part + 1))
                else:
                    dve.wait_ge(unit_used, PE_.unit(i, (part + 1) * PE_.n))
                src = MAIN[tt][:, 0:GC].rearrange("p (g d) -> p g d", g=G)
                a = rope_a[:, tt, :].rearrange("p (g d) -> p g d", g=G)
                b = rope_b[:, tt, :].rearrange("p (g d) -> p g d", g=G)
                H2 = HD // 2
                cos = cs_tab[:, tt, 0, :].unsqueeze(1).to_broadcast((P, G, HD))
                sin = cs_tab[:, tt, 1, :].unsqueeze(1).to_broadcast((P, G, HD))
                nc.vector.tensor_tensor(a, src, cos, ALU.mult).then_inc(rope_parts, 1)
                nc.vector.tensor_tensor(b[:, :, 0:H2], src[:, :, H2:HD], sin[:, :, 0:H2], ALU.mult).then_inc(rope_parts, 1)
                nc.vector.tensor_tensor(b[:, :, H2:HD], src[:, :, 0:H2], sin[:, :, H2:HD], ALU.mult).then_inc(d_free[tt], 1)
                dve.wait_ge(rope_parts, i * 8 + (2 * part + tt + 1) * 2)
                dve.wait_ge(d_free[tt], i * 3 + (part + 1))
                nc.vector.tensor_tensor(dst[:, tt, :].rearrange("p (g d) -> p g d", g=G), a, b, ALU.add).then_inc(roped, 1)

            def d_steps(ub, h, pos, second, third):
                if ub == pos["mask"]:
                    dve.wait_ge(scores_done, h + 1)
                    for src, n, at in ((Z[0], G * P, 0), (Z[1], 2 * SEQ, G * P), (third, SEQ, G * P + 2 * SEQ)):
                        nc.vector.scalar_tensor_tensor(out=sm[:, at:at + n], in0=src[:, 0:n], scalar=SCALE,
                                                       in1=mask_sb[:, at:at + n], op0=ALU.mult,
                                                       op1=ALU.add).then_inc(scores_masked, 1)
                if ub == pos["top"]:
                    dve.wait_ge(scores_masked, h * 3 + 3)
                    for t, cols in ((0, slice(0, G * P)), (1, slice(G * P, SC))):
                        nc.vector.tensor_reduce(mx[:, t:t + 1], sm[:, cols], AX.X, ALU.max, negate=True).then_inc(max_done, 1)
                if ub == pos["norm"]:
                    dve.wait_ge(p_done, h * 2 + 2)
                    nc.vector.reciprocal(rden[:, :], den[:, :]).then_inc(rden_done, 1)
                    dve.wait_ge(rden_done, h + 1)
                    for t, cols in ((0, slice(0, G * P)), (1, slice(G * P, SC))):
                        nc.vector.tensor_scalar(sm[:, cols], sm[:, cols], rden[:, t:t + 1], None,
                                                ALU.mult).then_inc(p_scaled, 1)
                if ub == pos["take"]:
                    dve.wait_ge(p_turned, h * 3 + 2)
                    nc.vector.tensor_copy(pT[:, 1, :], TRB[1][:, 0:TRI]).then_inc(pT_dve, 1)
                if ub == pos["lo"]:
                    dve.wait_ge(do_hi_done, h * 2 + 1)
                    two = bass.ds(h * G, 2)
                    nc.vector.tensor_tensor(ot_lo[:, two, :], second[:, :].rearrange("p (k n) -> p k n", k=2),
                                            ot_hi[:, two, :].bitcast(F32), ALU.subtract).then_inc(do_lo_done, 1)
                    dve.wait_ge(do_hi_done, h * 2 + 2)
                    one = bass.ds(h * G + 2, 1)
                    nc.vector.tensor_tensor(ot_lo[:, one, :].rearrange("p a n -> p (a n)"), third[:, 0:SEQ],
                                            ot_hi[:, one, :].rearrange("p a n -> p (a n)").bitcast(F32),
                                            ALU.subtract).then_inc(do_lo_done, 1)

            def d_body(i, first):
                for ub in range(PE_.nb):
                    if first:
                        if ub == 2:
                            y_take(PD, 1, OUTC - 1)
                        x_before(2, ub)
                    split(PE_, i, ub)
                    if not first:
                        if ub == 1:
                            stage(PE_.unit(i, 0), dv, GC, d_free)
                        d_steps(ub, i - 1, IN_BODY, YB[1], YB[0])
                    if first and ub == 10:
                        dve.wait_ge(tables_in, 32)
                    for part, dst in ((0, dq), (1, dk)):
                        for tt in range(TT):
                            if ub == 8 * part + 10 + tt - (not first):
                                rope_half(i, part, tt, dst)
                    if ub == 19:
                        dve.wait_ge(d_turned, i * 4 + 2)
                        nc.vector.tensor_copy(dqT[:, 2, :], TRB[1][:, 0:SEQ]).then_inc(d_turned_dve, 1)
                    if ub == 23:
                        dve.wait_ge(d_turned, i * 4 + 4)
                        nc.vector.tensor_copy(dkT[:, 2, :], TRB[1][:, 0:SEQ]).then_inc(d_turned_dve, 1)

            d_body(0, True)
            with dve.Fori(1, HPG) as i:
                d_body(i, False)
            for ub in range(PF.nb):
                split(PF, 0, ub)
                if ub == 1:
                    stage(PF.u0, dv, GC, d_free)
                d_steps(ub, HPG - 1, AT_END, MAIN[0], MAIN[1])
            y_rest(PF, 2)

            swiglu(PF, PG, PH, 1)

            y_take(PH, 3, OUTC - 1)
            moments(3)
            for q in range(OUTC):
                norm(3, q)
            dve.wait_ge(gb_in, 32 * 4)
            for q in range(1, OUTC):
                for tt in range(TT):
                    n = TT * (q - 1) + tt
                    part = resid[:, tt, q * COLS:(q + 1) * COLS]
                    dve.wait_ge(normed, 8 * 3 + TT * q + tt + 1)
                    nc.vector.tensor_tensor(part, part, gb_last[:, q * COLS:(q + 1) * COLS], ALU.mult).then_inc(out_scaled, 1)
                    dve.wait_ge(out_scaled, n + 1)
                    nc.vector.tensor_tensor(part, part, gb_last[:, D + q * COLS:D + (q + 1) * COLS],
                                            ALU.add).then_inc(out_ready, 1)

        @block.gpsimd
        def _(pool):
            def gb_load(ln, dst):
                for v, row in enumerate(gb_rows_of(ln)):
                    pool.dma_start(dst[:, v * D:(v + 1) * D], row.to_broadcast((P, D))).then_inc(gb_in, 16)

            def causal(buf, head, wait, value, done):
                pool.wait_ge(wait, value)
                v = buf[:, head % 2, :].rearrange("p (b t) -> p b t", b=3)[:, 0:3:2, :]
                nc.gpsimd.affine_select(out=v, in_=v, compare_op=ALU.is_gt, fill=0.0, base=0, pattern=[[0, 2], [1, P]],
                                        channel_multiplier=-1).then_inc(done, 1)

            def sb_masks(g, heads):
                for h in heads:
                    causal(s_buf, h, stay_done, g * GH + h + 1, stay_masked)
                    causal(w_buf, h, w_done, g * GH + h + 1, w_masked)

            def inv_sqrt(ln):
                pool.wait_ge(ln_veps, ln + 1)
                nc.gpsimd.tensor_tensor(rstd[:, :], veps[:, :], half[:, :], ALU.pow).then_inc(ln_rstd, 1)

            def residual(ln):
                pool.wait_ge(gb_in, 32 * (ln + 1))
                for q in range(OUTC):
                    pool.wait_ge(xt_turned, 8 * (ln + 1) + 2 * q + 2)
                    for tt in range(TT):
                        n = 8 * ln + TT * q + tt
                        part = resid[:, tt, q * COLS:(q + 1) * COLS]
                        nc.gpsimd.tensor_tensor(part, part, gb_flat[:, q * COLS:(q + 1) * COLS], ALU.mult).then_inc(scaled, 1)
                        pool.wait_ge(scaled, n + 1)
                        nc.gpsimd.tensor_tensor(part, part, gb_flat[:, D + q * COLS:D + (q + 1) * COLS],
                                                ALU.add).then_inc(resid_done, 1)

            nc.gpsimd.memset(half[:, :], -0.5).then_inc(half_set, 1)
            pool.wait_ge(half_set, 1)
            gb_load(0, gb_flat)
            for g in range(GROUPS - 1):
                sb_masks(g, range(GH))
            last = GROUPS - 1
            for a, b in ((0, 1), (2, 3)):
                for h in (a, b):
                    causal(s_buf, h, stay_done, GH * last + h + 1, stay_masked)
                for h in (a, b):
                    causal(w_buf, h, w_done, GH * last + h + 1, w_masked)
            inv_sqrt(0)
            residual(0)
            pool.wait_ge(unit_used, PE_.u0)
            gb_load(1, gb_flat)
            pool.dma_start(cs_tab, rope).then_inc(tables_in, 16)
            pool.dma_start(mask_sb, masks).then_inc(tables_in, 16)
            inv_sqrt(1)
            residual(1)
            pool.wait_ge(resid_done, 16)
            gb_load(2, gb_flat)
            inv_sqrt(2)
            residual(2)
            pool.wait_ge(unit_used, PH.u0)
            gb_load(3, gb_last)
            inv_sqrt(3)
            pool.wait_ge(gb_in, 32 * 4)
            for tt in range(TT):
                part = resid[:, tt, 0:COLS]
                pool.wait_ge(normed, 8 * 3 + tt + 1)
                nc.gpsimd.tensor_tensor(part, part, gb_last[:, 0:COLS], ALU.mult).then_inc(out_scaled_pool, 1)
                pool.wait_ge(out_scaled_pool, tt + 1)
                nc.gpsimd.tensor_tensor(part, part, gb_last[:, D:D + COLS], ALU.add).then_inc(out_ready_pool, 1)


def shape_constants():
    j = np.arange(P)
    tri = np.stack([np.eye(P), -(j[:, None] >= j[None, :]).astype(float), -np.ones((P, P))], 1).astype(np.float32)
    pos = np.arange(SEQ, dtype=np.float32)
    inv = np.float32(THETA) ** (-np.arange(0, HD, 2, dtype=np.float32) / np.float32(HD))
    ang = pos[:, None] * inv[None, :]
    cos, sin = np.cos(ang), np.sin(ang)
    table = np.stack([np.concatenate([cos, cos], 1), np.concatenate([-sin, sin], 1)], 1)
    rope = np.ascontiguousarray(table.reshape(TT, P, 2, HD).transpose(1, 0, 2, 3)).astype(np.float32)
    blocks = []
    for t0, keys in ((0, P), (P, SEQ)):
        for window, dilation in DIL:
            back = (t0 + np.arange(P))[:, None] - np.arange(keys)[None, :]
            valid = (back >= 0) & (back % dilation == 0) & (back <= window)
            blocks.append(np.where(valid, 0.0, NEG))
    return tri, rope, np.concatenate(blocks, 1).astype(np.float32)


_INS = ["x", "w_qkv_sb", "w_o_sb", "w_qkv_dil", "w_o_dil", "ln_mix_g", "ln_mix_b", "w_gate_up", "w_down", "ln_ffn_g",
        "ln_ffn_b"]


def kernel(**inputs):
    import concourse.bacc as bacc
    from concourse.bass_utils import run_bass_kernel_spmd

    nc = bacc.Bacc("TRN2", target_bir_lowering=False, num_devices=1)
    arrays, args = {}, []
    tri, rope, masks = shape_constants()
    for name, a in [(n, np.ascontiguousarray(inputs[n])) for n in _INS] + [("tri", tri), ("rope", rope), ("masks", masks)]:
        arrays[f"in_{name}"] = a
        args.append(nc.dram_tensor(f"in_{name}", a.shape, mybir.dt.from_np(a.dtype), kind="ExternalInput").ap())
    args.append(nc.dram_tensor("out_0", (1, SEQ, D), F32, kind="ExternalOutput").ap())
    build(nc, *args)
    r = run_bass_kernel_spmd(nc, [arrays], core_ids=[0])
    return r.results[0]["out_0"]
```

```python
import math
from contextlib import ExitStack

import numpy as np
import concourse.bass as bass
from concourse import mybir

F32 = mybir.dt.float32
F32R = mybir.dt.float32r
ALU = mybir.AluOpType
ACT = mybir.ActivationFunctionType
AX = mybir.AxisListType

P = 128
SEQ = 256
TT = SEQ // P
D = 2048
KT = D // P
HD = 128
SB_HEADS = D // HD
DIL = ((128, 1), (512, 4), (2048, 16))
G = len(DIL)
HPG = 6
DIL_HEADS = G * HPG
FF = -(-(8 * D) // (3 * 256)) * 256
FKT = FF // P
DEPTH = 2
ALPHA = (2.0 * DEPTH) ** 0.25
EPS = 1e-5
SCALE = 1.0 / math.sqrt(HD)
THETA = 10000.0
COLS = 512
GH = COLS // HD
GROUPS = SB_HEADS // GH
PAIRS = FF // COLS
OUTC = D // COLS
NEG = -1e30
PIECES = TT * OUTC
POOL_PIECES = 2
OUT_ORDER = (2, 0, 3, 4, 1, 5, 6, 7)
SLOTS = 4


class Phase:

    def __init__(self, prev, bodies, cpb, nk, units_per_load, ncols, inc=16, slots=None):
        self.prev, self.bodies, self.cpb, self.nk, self.ncols, self.inc = prev, bodies, cpb, nk, ncols, inc
        self.n = len(nk)
        self.nb = self.n * cpb
        self.k0 = [sum(nk[:u]) for u in range(self.n)]
        self.slot = slots or [u % SLOTS for u in range(self.n)]
        self.load = []
        for l, c in enumerate(units_per_load):
            self.load += [l] * c
        self.loads = len(units_per_load)
        self.first_of = [self.load.index(l) for l in range(self.loads)]
        self.end_of = [self.first_of[l] + units_per_load[l] for l in range(self.loads)]
        self.fills = [sum(l % SLOTS == s for l in range(self.loads)) for s in range(SLOTS)]
        self.u0 = prev.u0 + prev.bodies * prev.nb if prev else 0
        self.c0 = prev.c0 + prev.bodies * prev.cpb if prev else 0
        self.f0 = [prev.f0[s] + prev.fills[s] * prev.inc * prev.bodies * prev.cpb if prev else 0 for s in range(SLOTS)]

    def unit(self, body, ub):
        return body * self.nb + self.u0 + ub

    def chunk(self, body, ub):
        return body * self.cpb + self.c0 + ub // self.n

    def filled(self, body, ub):
        l = self.load[ub % self.n]
        s = l % SLOTS
        c = body * self.cpb + ub // self.n
        return c * (self.fills[s] * self.inc) + self.f0[s] + (l // SLOTS + 1) * self.inc

    def ring_before(self, body, ub, first):
        u, start = ub % self.n, self.unit(body, ub - ub % self.n)
        mine = [v for v in range(u) if self.slot[v] == self.slot[u]]
        if mine:
            return start + mine[-1] + 1
        before = self.prev if first and ub < self.n else self
        if before is None:
            return None
        last = [v for v in range(before.n) if before.slot[v] == self.slot[u]][-1]
        return start - before.n + last + 1

    def raw_before(self, body, cb, l, first):
        start = self.unit(body, cb * self.n)
        if l >= SLOTS:
            return start + self.end_of[l - SLOTS]
        before = self.prev if first and cb == 0 else self
        if before is None:
            return None
        last = [m for m in range(before.loads) if m % SLOTS == l % SLOTS][-1]
        return start - before.n + before.end_of[last]


TWO8 = [2] * 8
PA = Phase(None, GROUPS, 3, TWO8, [2] * 4, COLS)
PB = Phase(PA, OUTC, 1, TWO8, [2] * 4, COLS)
PC = Phase(PB, PAIRS, 2, TWO8, [2] * 4, COLS)
DOWN_SLOTS = [u % SLOTS for u in range(FKT // 2 - 2)] + [2, 3]
PD = Phase(PC, OUTC, 1, [2] * (FKT // 2), [2] * (FKT // 4), COLS, slots=DOWN_SLOTS)
PE_ = Phase(PD, HPG, 3, TWO8, [2] * 4, G * HD, inc=16 * G)
PF = Phase(PE_, OUTC, 1, [2, 1] * HPG, [2] * HPG, COLS)
PG = Phase(PF, PAIRS, 2, TWO8, [2] * 4, COLS)
PH = Phase(PG, OUTC, 1, [2] * (FKT // 2), [2] * (FKT // 4), COLS, slots=DOWN_SLOTS)


def build(nc, x, w_qkv_sb, w_o_sb, w_qkv_dil, w_o_dil, ln_mix_g, ln_mix_b, w_gate_up, w_down, ln_ffn_g, ln_ffn_b,
          tri, rope, masks, out):
    ctx = ExitStack()
    with ctx:
        def sb(name, shape, dt=F32):
            return ctx.enter_context(nc.sbuf_tensor(name, shape, dt))

        def sem(name):
            return ctx.enter_context(nc.semaphore(name))

        resid = sb("resid", [P, TT, D])
        xt_at = (nc.sbuf_base + 31) // 32 * 32
        xt_hi = sb("xt_hi", [P, KT, SEQ], F32R)
        xt_lo = sb("xt_lo", [P, KT, SEQ], F32R)
        raw = sb("raw", [P, SLOTS, 4 * COLS])
        w_hi = sb("w_hi", [P, SLOTS, 2 * COLS], F32R)
        w_lo = sb("w_lo", [P, SLOTS, 2 * COLS], F32R)
        stg = sb("stg", [P, TT, COLS])
        consts = sb("consts", [P, 3, P])
        gbT = sb("gbT", [P, P])
        stats = sb("stats", [P, TT, OUTC, 6])
        mv = sb("mv", [P, TT, 2])
        veps = sb("veps", [P, TT])
        half = sb("half", [P, TT])
        rstd = sb("rstd", [P, TT])
        mx = sb("mx", [P, TT])
        den = sb("den", [P, TT])
        rden = sb("rden", [P, TT])
        arena_bytes = FKT * SEQ * 4
        arena = (nc.sbuf_base + 31) // 32 * 32
        assert arena + 2 * arena_bytes <= nc.sbuf_usable_end

        def placed(name, shape, dt, at):
            return nc.alloc_sbuf_tensor_at(name, shape, dt, offset=at)

        arena_hi = placed("arena_hi", [P, FKT, SEQ], F32R, arena)
        arena_lo = placed("arena_lo", [P, FKT, SEQ], F32R, arena + arena_bytes)
        ident, negtri, negones = consts[:, 0, :], consts[:, 1, :], consts[:, 2, :]
        ot_hi = arena_hi[:, 0:DIL_HEADS, :]
        ot_lo = arena_lo[:, 0:DIL_HEADS, :]
        ot_bytes = DIL_HEADS * SEQ * 4
        n_rest = (FKT - DIL_HEADS) * SEQ
        n_more = n_rest - 2 * D
        rest = placed("mixer_bufs", [P, n_rest], F32, arena + ot_bytes)
        more = placed("mixer_bufs2", [P, n_more], F32, arena + arena_bytes + ot_bytes)
        gb_flat = placed("gb_everywhere", [P, 2 * D], F32, arena + 2 * arena_bytes - 8 * D)
        gb_last = placed("gb_last", [P, 2 * D], F32, xt_at)

        def carve(region, at, *shape):
            n = math.prod(shape)
            v = region[:, at:at + n]
            if len(shape) == 2:
                v = v.rearrange("p (a b) -> p a b", a=shape[0])
            if len(shape) == 3:
                v = v.rearrange("p (a b c) -> p a b c", a=shape[0], b=shape[1])
            return v, at + n

        sq, at = carve(rest, 0, TT, COLS)
        sk, at = carve(rest, at, TT, COLS)
        sv, at = carve(rest, at, TT, COLS)
        qT, at = carve(rest, at, GH, SEQ)
        kT, at = carve(rest, at, GH, SEQ)
        TRI = SEQ + P
        ew_buf, at = carve(rest, at, GH, TRI)
        assert at <= n_rest
        s_buf, at = carve(more, 0, GH, TRI)
        gb_rows, at = carve(more, at, P)
        assert at <= n_more
        GC = G * HD
        dq, at = carve(rest, 0, TT, GC)
        dk, at = carve(rest, at, TT, GC)
        dv, at = carve(rest, at, TT, GC)
        dqT, at = carve(rest, at, G, SEQ)
        dkT, at = carve(rest, at, G, SEQ)
        SC = G * P + G * SEQ
        sm, at = carve(rest, at, SC)
        cs_tab, at = carve(rest, at, TT, 2, HD)
        pT, at = carve(rest, at, G, TRI)
        assert at <= n_rest
        mask_sb, at = carve(more, 0, SC)
        rope_a, at = carve(more, at, TT, GC)
        assert at <= n_more
        rope_b = stg[:, :, 0:GC]

        bank = [ctx.enter_context(nc.psum_tensor(f"bank{i}", [P, COLS], F32)) for i in range(8)]
        MAIN, UP, TRB, YB = bank[0:2], bank[2:4], bank[4:6], bank[6:8]
        Z = UP
        Z4 = UP + TRB

        consts_in = sem("consts_in")
        x_in = [sem(f"x_in{q}") for q in range(OUTC)]
        rows_in = sem("rows_in")
        gb_in = sem("gb_in")
        tables_in = sem("tables_in")
        gbT_made = sem("gbT_made")
        gbT_ready = sem("gbT_ready")
        half_set = sem("half_set")
        raw_full = [sem(f"raw_full{s}") for s in range(SLOTS)]
        hi_done = sem("hi_done")
        lo_done = sem("lo_done")
        unit_used = sem("unit_used")
        tt0_done = sem("tt0_done")
        xt_turned = sem("xt_turned")
        xt_read = sem("xt_read")
        xt_hi_done = sem("xt_hi_done")
        xt_lo_done = sem("xt_lo_done")
        y_added = sem("y_added")
        y_stats = sem("y_stats")
        ln_mean = sem("ln_mean")
        ln_veps = sem("ln_veps")
        ln_rstd = sem("ln_rstd")
        normed = sem("normed")
        scaled = sem("scaled")
        resid_done = sem("resid_done")
        out_scaled = sem("out_scaled")
        out_scaled_pool = sem("out_scaled_pool")
        out_ready = sem("out_ready")
        out_ready_pool = sem("out_ready_pool")
        out_sent = sem("out_sent")
        sb_free = [sem("sb_free0"), sem("sb_free1")]
        turned = sem("turned")
        turned_act = sem("turned_act")
        turned_dve = sem("turned_dve")
        z_done = sem("z_done")
        abs_done = sem("abs_done")
        exp_done = sem("exp_done")
        log_done = sem("log_done")
        stay_done = sem("stay_done")
        stay_masked = sem("stay_masked")
        later_done = sem("later_done")
        w_done = sem("w_done")
        w_masked = sem("w_masked")
        o_done = sem("o_done")
        o_hi_done = sem("o_hi_done")
        o_free = sem("o_free")
        d_free = [sem("d_free0"), sem("d_free1")]
        rope_parts = sem("rope_parts")
        roped = sem("roped")
        d_turned = sem("d_turned")
        d_turned_act = sem("d_turned_act")
        d_turned_dve = sem("d_turned_dve")
        scores_done = sem("scores_done")
        scores_masked = sem("scores_masked")
        max_done = sem("max_done")
        p_done = sem("p_done")
        rden_done = sem("rden_done")
        p_scaled = sem("p_scaled")
        p_turned = sem("p_turned")
        pT_act = sem("pT_act")
        pT_dve = sem("pT_dve")
        do_done = sem("do_done")
        do_hi_done = sem("do_hi_done")
        do_lo_done = sem("do_lo_done")
        silu_done = [sem(f"silu_done{l}") for l in range(DEPTH)]
        h_done = [sem(f"h_done{l}") for l in range(DEPTH)]
        h_turned = [sem(f"h_turned{l}") for l in range(DEPTH)]
        ht_hi_done = [sem(f"ht_hi_done{l}") for l in range(DEPTH)]
        ht_lo_done = [sem(f"ht_lo_done{l}") for l in range(DEPTH)]

        FREE = 2

        IN_BODY = dict(score=1, mask=3, top=4, exp=5, norm=6, turn=9, take=11, turn2=12, take2=14, pv=15, hi=17, lo=18)
        AT_END = dict(score=1, mask=3, top=3, exp=4, norm=5, turn=6, take=7, turn2=8, take2=9, pv=9, hi=10, lo=10)

        WARM_STATS, WARM_NORM, WARM_SPLIT, WARM_START = 20, 6, 10, 10

        def x_rounds(ev, ub):
            if ev == 0:
                return [ub] if ub < KT // 2 else []
            return [0, 1] if ub == 3 else [ub - 2] if 3 < ub < KT // 2 + 2 else []

        rows_k = "(k p) n -> p k n"

        def gb_col(ln, which, kt):
            return (ln % 2) * 64 + which * 32 + (ln // 2) * KT + kt

        def gb_rows_of(ln):
            gain, bias = (ln_mix_g, ln_mix_b) if ln % 2 == 0 else (ln_ffn_g, ln_ffn_b)
            return gain[ln // 2:ln // 2 + 1, :], bias[ln // 2:ln // 2 + 1, :]

        block = ctx.enter_context(nc.Block())

        @block.sync
        def _(sp):
            def load(ph, body, cb, l, first, source):
                before = ph.raw_before(body, cb, l, first)
                if before is not None:
                    sp.wait_ge(lo_done, before)
                u = ph.first_of[l]
                k0, nk = ph.k0[u], sum(ph.nk[u:ph.end_of[l]])
                dst = raw[:, l % SLOTS, 0:nk * ph.ncols].rearrange("p (k n) -> p k n", k=nk)
                for d, s in source(body, cb, l, k0, nk, dst):
                    sp.dma_start(d, s).then_inc(raw_full[l % SLOTS], 16)

            def walk(ph, source):
                for cb in range(ph.cpb):
                    for l in range(ph.loads):
                        load(ph, 0, cb, l, True, source)
                with sp.Fori(1, ph.bodies) as i:
                    for cb in range(ph.cpb):
                        for l in range(ph.loads):
                            load(ph, i, cb, l, False, source)

            def plain(w, col):
                def source(body, cb, l, k0, nk, dst):
                    rows = w[k0 * P:(k0 + nk) * P, bass.ds(col(body, cb), COLS)]
                    return [(dst, rows.rearrange(rows_k, p=P))]
                return source

            def dilated_qkv(body, cb, l, k0, nk, dst):
                for g in range(G):
                    col = body * HD + (cb * DIL_HEADS + g * HPG) * HD
                    rows = w_qkv_dil[0, k0 * P:(k0 + nk) * P, bass.ds(col, HD)]
                    yield dst[:, :, g * HD:(g + 1) * HD], rows.rearrange(rows_k, p=P)

            def dilated_out(body, cb, l, k0, nk, dst):
                by_head = w_o_dil[0].rearrange("(g h p) n -> h p g n", g=G, h=HPG)
                return [(dst, by_head[l, :, :, bass.ds(body * COLS, COLS)])]

            sp.dma_start(consts[:, :, :], tri).then_inc(consts_in, 16)
            for q in range(OUTC):
                sp.dma_start(resid[:, :, q * COLS:(q + 1) * COLS],
                             x[0, :, q * COLS:(q + 1) * COLS].rearrange("(t p) d -> p t d", p=P)).then_inc(x_in[q], 16)
                load(PA, 0, 0, q, True, plain(w_qkv_sb[0], lambda body, cb: 0))
            for v, rows in enumerate((ln_mix_g, ln_mix_b, ln_ffn_g, ln_ffn_b)):
                sp.dma_start(gb_rows[v * 2 * KT:(v + 1) * 2 * KT, :],
                             rows.rearrange("l (k p) -> (l k) p", p=P)).then_inc(rows_in, 16)
            qkv_sb = plain(w_qkv_sb[0], lambda body, cb: body * COLS + cb * D)
            for cb in range(1, PA.cpb):
                for l in range(PA.loads):
                    load(PA, 0, cb, l, True, qkv_sb)
            with sp.Fori(1, PA.bodies) as i:
                for cb in range(PA.cpb):
                    for l in range(PA.loads):
                        load(PA, i, cb, l, False, qkv_sb)
            walk(PB, plain(w_o_sb[0], lambda body, cb: body * COLS))
            walk(PC, plain(w_gate_up[0], lambda body, cb: body * COLS + cb * FF))
            walk(PD, plain(w_down[0], lambda body, cb: body * COLS))
            walk(PE_, dilated_qkv)
            walk(PF, dilated_out)
            walk(PG, plain(w_gate_up[1], lambda body, cb: body * COLS + cb * FF))
            walk(PH, plain(w_down[1], lambda body, cb: body * COLS))
            for n in OUT_ORDER:
                if n < POOL_PIECES:
                    sp.wait_ge(out_ready_pool, n + 1)
                else:
                    sp.wait_ge(out_ready, n - POOL_PIECES + 1)
                tt, cols = n % TT, slice(n // TT * COLS, (n // TT + 1) * COLS)
                sp.dma_start(out[0, tt * P:(tt + 1) * P, cols], resid[:, tt, cols]).then_inc(out_sent, 16)
            sp.wait_ge(out_sent, 16 * PIECES)

        @block.tensor
        def _(pe):
            def unit(ph, body, ub, a_hi, a_lo, banks, free=None):
                u, w = ub % ph.n, ph.ncols
                pe.wait_ge(lo_done, ph.unit(body, ub) + 1)
                for tt in range(TT):
                    if free is not None:
                        pe.wait_ge(*free[tt])
                    for kk in range(ph.nk[u]):
                        col = slice(kk * w, (kk + 1) * w)
                        terms = ((a_hi, w_hi), (a_hi, w_lo), (a_lo, w_hi))
                        for n, (a, b) in enumerate(terms):
                            mm = nc.tensor.matmul(banks[tt][:, 0:w], a[:, ph.k0[u] + kk, tt * P:(tt + 1) * P],
                                                  b[:, ph.slot[u], col], start=(u == 0 and kk == 0 and n == 0),
                                                  stop=(u == ph.n - 1 and kk == ph.nk[u] - 1 and n == 2))
                    if tt == 0 and u == ph.n - 1:
                        mm.then_inc(tt0_done, 1)
                mm.then_inc(unit_used, 1)

            def turn_x(ev, r):
                if ev == 0:
                    pe.wait_ge(x_in[r // 2], 16)
                else:
                    pe.wait_ge(normed, 8 * (ev - 1) + 2 * (r // 2) + 2)
                if r >= 2:
                    pe.wait_ge(xt_read, 8 * ev + r - 1)
                for kk in range(2):
                    for tt in range(TT):
                        k = 2 * r + kk
                        t = nc.tensor.transpose(TRB[r % 2][:, (2 * kk + tt) * P:(2 * kk + tt + 1) * P],
                                                resid[:, tt, k * P:(k + 1) * P], ident)
                t.then_inc(xt_turned, 1)

            def keep_warm(n):
                for _ in range(n):
                    nc.tensor.transpose(UP[0][:, 0:P], ident, ident)

            def x_before(ev, ub):
                if ub == 0:
                    if ev > 0:
                        keep_warm(WARM_STATS)
                        pe.wait_ge(ln_veps, ev)
                        keep_warm(WARM_NORM)
                    turn_x(ev, 0)
                    turn_x(ev, 1)
                    keep_warm(WARM_START if ev == 0 else WARM_SPLIT)
                if ub < KT // 2 - 2:
                    turn_x(ev, ub + 2)
                if ub < KT // 2:
                    pe.wait_ge(xt_lo_done, 8 * ev + ub + 1)

            def sb_scores(g, h, z):
                pe.wait_ge((turned_act, turned_dve)[h // 2], g * 2 + 2)
                nc.tensor.matmul(z[:, 0:SEQ], kT[:, h, 0:P], qT[:, h, :], start=True, stop=True,
                                 skip_group_check=True)
                nc.tensor.matmul(z[:, SEQ:TRI], kT[:, h, P:SEQ], qT[:, h, P:SEQ], start=False, stop=True,
                                 skip_group_check=True).then_inc(z_done, 1)

            def sb_later(g, h, z):
                pe.wait_ge(stay_masked, g * GH + h + 1)
                nc.tensor.matmul(z[:, 0:TRI], negtri, s_buf[:, h, :], start=False, stop=True,
                                 skip_group_check=True)
                nc.tensor.matmul(z[:, P:SEQ], negones, s_buf[:, h, SEQ:TRI], start=False, stop=True,
                                 skip_group_check=True).then_inc(later_done, 1)

            def sb_values(g, h, o, free=None):
                pe.wait_ge(w_masked, g * GH + h + 1)
                pe.wait_ge(sb_free[0], g * 3 + 3)
                pe.wait_ge(sb_free[1], g * 3 + 3)
                if free is not None:
                    pe.wait_ge(o_free, free)
                cols = slice(h * HD, (h + 1) * HD)
                nc.tensor.matmul(o[:, 0:SEQ], sv[:, 0, cols], ew_buf[:, h, 0:SEQ], start=True, stop=False,
                                 skip_group_check=True)
                nc.tensor.matmul(o[:, P:SEQ], sv[:, 1, cols], ew_buf[:, h, SEQ:TRI], start=False,
                                 stop=True, skip_group_check=True).then_inc(o_done, 1)

            def sb_turn(i, part, src):
                for tt in range(TT):
                    pe.wait_ge(sb_free[tt], i * 3 + part + 1)
                if part == 1:
                    pe.wait_ge(turned_act, i * 2 + 1)
                    pe.wait_ge(turned_dve, i * 2 + 1)
                for h in range(GH):
                    for tt in range(TT):
                        at = (h % 2) * SEQ + tt * P
                        t = nc.tensor.transpose(TRB[h // 2][:, at:at + P], src[:, tt, h * HD:(h + 1) * HD], ident)
                    if h % 2:
                        t.then_inc(turned, 1)

            def sb_body(i, first):
                for ub in range(PA.nb):
                    part = ub // PA.n
                    if first and part == 0:
                        x_before(0, ub)
                    free = None
                    if ub % PA.n == 0 and not (first and part == 0):
                        free = [(sb_free[tt], i * 3 + part) for tt in range(TT)]
                    unit(PA, i, ub, xt_hi, xt_lo, MAIN, free)
                    if first and ub == 9:
                        pe.wait_ge(rows_in, 64)
                        nc.tensor.transpose(YB[1][:, 0:P], gb_rows[:, :], ident).then_inc(gbT_made, 1)
                    if not first:
                        h, step = divmod(ub - 1, 4)
                        if ub >= 1 and step == 0 and h < GH:
                            sb_scores(i - 1, h, Z[h % 2])
                        h, step = divmod(ub - 4, 4)
                        if ub >= 4 and step == 0 and h < GH:
                            sb_later(i - 1, h, Z[h % 2])
                        h, step = divmod(ub - 7, 4)
                        if ub >= 7 and step == 0 and h < GH:
                            sb_values(i - 1, h, YB[h % 2], free=(i - 1) * GH + h + 1)
                    if ub == 17:
                        sb_turn(i, 0, sq)
                    if ub == 20:
                        sb_turn(i, 1, sk)

            pe.wait_ge(consts_in, 16)
            sb_body(0, True)
            with pe.Fori(1, GROUPS) as i:
                sb_body(i, False)

            def y_chunk(ph, ln, c, a_hi, a_lo, first, ub):
                free = None
                if ub == 0 and not first:
                    free = [(y_added, c * 2 + (8 * ln - 1 + tt)) for tt in range(TT)]
                unit(ph, c, ub, a_hi, a_lo, YB, free)

            def y_rest(ph, ln, a_hi, a_lo):
                with pe.Fori(1, OUTC) as c:
                    for ub in range(ph.nb):
                        y_chunk(ph, ln, c, a_hi, a_lo, False, ub)

            last = GROUPS - 1
            pe.wait_ge(o_free, GH * last + FREE)
            pe.wait_ge(turned_act, GROUPS * 2)
            pe.wait_ge(turned_dve, GROUPS * 2)
            for h in range(GH):
                sb_scores(last, h, Z4[h])
            for ub in range(PB.nb):
                if ub >= 6:
                    pe.wait_ge(o_free, GH * last + FREE + 2 * (ub - 6) + 2)
                y_chunk(PB, 0, 0, ot_hi, ot_lo, True, ub)
                for h in range(GH):
                    if ub == 3:
                        sb_later(last, h, Z4[h])
                    if ub == 4:
                        sb_values(last, h, MAIN[h // 2][:, (h % 2) * SEQ:(h % 2 + 1) * SEQ])
            y_rest(PB, 0, ot_hi, ot_lo)

            def turn_h(l, c):
                pe.wait_ge(h_done[l], c * 2 + 2)
                pe.wait_ge(ht_lo_done[l], c * 2 + FREE)
                for r in range(2):
                    for kk in range(2):
                        for tt in range(TT):
                            k = 2 * r + kk
                            t = nc.tensor.transpose(TRB[r][:, (2 * kk + tt) * P:(2 * kk + tt + 1) * P],
                                                    stg[:, tt, k * P:(k + 1) * P], ident)
                    t.then_inc(h_turned[l], 1)

            def pair(ph, l, ev, c, first):
                for ub in range(ph.nb):
                    if first:
                        x_before(ev, ub)
                    banks = (MAIN, UP)[ub // ph.n]
                    free = None
                    if ub % ph.n == 0 and not first:
                        read = (silu_done, h_done)[ub // ph.n][l]
                        free = [(read, c * 2 - 1 + tt) for tt in range(TT)]
                    unit(ph, c, ub, xt_hi, xt_lo, banks, free)
                    if ub == 4 and not first:
                        turn_h(l, c - 1)

            def swiglu(pg, pd, l):
                ev = 2 * l + 1
                pair(pg, l, ev, 0, True)
                with pe.Fori(1, PAIRS) as c:
                    pair(pg, l, ev, c, False)
                for ub in range(pd.nb):
                    if ub == 0:
                        pe.wait_ge(ht_lo_done[l], 2 * (PAIRS - 1) + FREE)
                    if ub >= pd.nb - 2:
                        pe.wait_ge(ht_lo_done[l], 2 * (PAIRS - 1) + ub - (pd.nb - 2) + 1 + FREE)
                    y_chunk(pd, 2 * l + 1, 0, arena_hi, arena_lo, True, ub)
                    if ub == 4:
                        turn_h(l, PAIRS - 1)
                y_rest(pd, 2 * l + 1, arena_hi, arena_lo)

            swiglu(PC, PD, 0)

            def d_turn(i, part, src):
                pe.wait_ge(roped, i * 4 + 2 * part + 2)
                if part == 1:
                    pe.wait_ge(d_turned_act, i * 2 + 1)
                    pe.wait_ge(d_turned_dve, i * 2 + 1)
                for g in range(G):
                    for tt in range(TT):
                        at = (g % 2) * SEQ + tt * P
                        t = nc.tensor.transpose(TRB[g // 2][:, at:at + P], src[:, tt, g * HD:(g + 1) * HD], ident)
                    if g >= 1:
                        t.then_inc(d_turned, 1)

            def d_steps(ub, h, pos, second, third):
                if ub == pos["score"]:
                    pe.wait_ge(d_turned_act, h * 2 + 2)
                    pe.wait_ge(d_turned_dve, h * 2 + 2)
                    pe.wait_ge(do_lo_done, h * 2 + FREE)
                    for g in range(G):
                        nc.tensor.matmul(Z[0][:, g * P:(g + 1) * P], dqT[:, g, 0:P], dkT[:, g, 0:P], start=True,
                                         stop=True)
                    for g in range(2):
                        nc.tensor.matmul(Z[1][:, g * SEQ:(g + 1) * SEQ], dqT[:, g, P:SEQ], dkT[:, g, :], start=True,
                                         stop=True)
                    nc.tensor.matmul(third[:, 0:SEQ], dqT[:, 2, P:SEQ], dkT[:, 2, :], start=True,
                                     stop=True).then_inc(scores_done, 1)
                if ub == pos["turn"]:
                    pe.wait_ge(p_scaled, h * 2 + 2)
                for g in range(G):
                    if ub == pos["turn2" if g == 2 else "turn"]:
                        if g == 2:
                            pe.wait_ge(pT_act, h * 2 + 1)
                        for n, at in enumerate((g * P, G * P + g * SEQ, G * P + g * SEQ + P)):
                            t = nc.tensor.transpose(TRB[g % 2][:, n * P:(n + 1) * P], sm[:, at:at + P], ident)
                        t.then_inc(p_turned, 1)
                if ub == pos["pv"]:
                    pe.wait_ge(pT_act, h * 2 + 2)
                    pe.wait_ge(pT_dve, h + 1)
                    for tt in range(TT):
                        pe.wait_ge(d_free[tt], h * 3 + 3)
                    for g in range(G):
                        dst, at = (second, g * SEQ) if g < 2 else (third, 0)
                        cols = slice(g * HD, (g + 1) * HD)
                        nc.tensor.matmul(dst[:, at:at + SEQ], dv[:, 0, cols], pT[:, g, 0:SEQ], start=True, stop=False,
                                         skip_group_check=True)
                        t = nc.tensor.matmul(dst[:, at + P:at + SEQ], dv[:, 1, cols], pT[:, g, SEQ:TRI], start=False,
                                             stop=True, skip_group_check=True)
                        if g >= 1:
                            t.then_inc(do_done, 1)

            def d_body(i, first):
                for ub in range(PE_.nb):
                    part = ub // PE_.n
                    if first and part == 0:
                        x_before(2, ub)
                    free = None
                    if ub % PE_.n == 0 and not (first and part == 0):
                        free = [(d_free[tt], i * 3 + part) for tt in range(TT)]
                    unit(PE_, i, ub, xt_hi, xt_lo, MAIN, free)
                    if not first:
                        d_steps(ub, i - 1, IN_BODY, YB[1], YB[0])
                    if ub == 17:
                        d_turn(i, 0, dq)
                    if ub == 21:
                        d_turn(i, 1, dk)

            d_body(0, True)
            with pe.Fori(1, HPG) as i:
                d_body(i, False)
            pe.wait_ge(do_lo_done, 2 * (HPG - 1) + FREE)
            for ub in range(PF.nb):
                if ub == AT_END["hi"]:
                    pe.wait_ge(do_lo_done, 2 * HPG + FREE)
                y_chunk(PF, 2, 0, ot_hi, ot_lo, True, ub)
                if ub == AT_END["score"]:
                    for tt in range(TT):
                        pe.wait_ge(d_free[tt], 3 * HPG)
                d_steps(ub, HPG - 1, AT_END, MAIN[0], MAIN[1])
            y_rest(PF, 2, ot_hi, ot_lo)

            swiglu(PG, PH, 1)

        @block.scalar
        def _(act):
            def split(ph, body, ub, first):
                u = ub % ph.n
                l = ph.load[u]
                if u == ph.first_of[l]:
                    act.wait_ge(raw_full[l % SLOTS], ph.filled(body, ub))
                before = ph.ring_before(body, ub, first)
                if before is not None:
                    act.wait_ge(unit_used, before)
                at, n = (ph.k0[u] - ph.k0[ph.first_of[l]]) * ph.ncols, ph.nk[u] * ph.ncols
                nc.scalar.activation(w_hi[:, ph.slot[u], 0:n], raw[:, l % SLOTS, at:at + n], ACT.Copy).then_inc(hi_done, 1)

            def x_round(ev, r):
                act.wait_ge(xt_turned, 8 * ev + r + 1)
                if r >= 2:
                    act.wait_ge(xt_lo_done, 8 * ev + r - 1)
                tmp = stg[:, r % 2, :]
                if ev == 0:
                    nc.scalar.activation(tmp, TRB[r % 2][:, :], ACT.Copy).then_inc(xt_read, 1)
                else:
                    for kk in range(2):
                        g, b = (gb_col(ev - 1, v, 2 * r + kk) for v in range(2))
                        a = nc.scalar.activation(tmp[:, kk * SEQ:(kk + 1) * SEQ], TRB[r % 2][:, kk * SEQ:(kk + 1) * SEQ],
                                                 ACT.Identity, bias=gbT[:, b:b + 1], scale=gbT[:, g:g + 1])
                    a.then_inc(xt_read, 1)

            def x_before(ev, ub):
                for r in x_rounds(ev, ub):
                    x_round(ev, r)

            def stage(tt0_chunk, dst, width, free):
                act.wait_ge(tt0_done, tt0_chunk + 1)
                nc.scalar.activation(dst[:, 0, :], MAIN[0][:, 0:width], ACT.Copy).then_inc(free[0], 1)

            def sb_abs_exp(g, heads, z):
                for h in heads:
                    act.wait_ge(z_done, g * GH + h + 1)
                    nc.scalar.activation(ew_buf[:, h, :], z[h][:, 0:TRI], ACT.Abs).then_inc(abs_done, 1)
                for h in heads:
                    act.wait_ge(abs_done, g * GH + h + 1)
                    nc.scalar.activation(ew_buf[:, h, :], ew_buf[:, h, :], ACT.Exp, scale=-1.0).then_inc(exp_done, 1)

            def sb_log(g, heads):
                for h in heads:
                    act.wait_ge(exp_done, g * GH + h + 1)
                    nc.scalar.activation(ew_buf[:, h, :], ew_buf[:, h, :], ACT.Ln, bias=1.0).then_inc(log_done, 1)

            def sb_weights(g, h, z):
                act.wait_ge(later_done, g * GH + h + 1)
                nc.scalar.activation(ew_buf[:, h, :], z[:, 0:TRI], ACT.Exp).then_inc(w_done, 1)

            def sb_out(g, h, n, bank):
                act.wait_ge(o_done, g * GH + h + n)
                nc.scalar.activation(ot_hi[:, bass.ds(g * GH + h, n), :], bank[:, 0:n * SEQ].rearrange(
                    "p (a t) -> p a t", a=n), ACT.Copy).then_inc(o_hi_done, n)

            def sb_body(i, first):
                for ub in range(PA.nb):
                    if first:
                        x_before(0, ub)
                    split(PA, i, ub, first)
                    if first and ub == 12:
                        act.wait_ge(gbT_made, 1)
                        nc.scalar.activation(gbT[:, :], YB[1][:, 0:P], ACT.Copy).then_inc(gbT_ready, 1)
                    if ub == (10 if first else 8):
                        stage(i * 3 + PA.c0, sq, COLS, sb_free)
                    if ub == 16:
                        stage(i * 3 + (PA.c0 + 1), sk, COLS, sb_free)
                    if not first:
                        if ub == 1:
                            stage(i * 3 + (PA.c0 - 1), sv, COLS, sb_free)
                        h, step = divmod(ub - 3, 4)
                        if ub >= 3 and step == 0 and h < GH:
                            sb_abs_exp(i - 1, [h], {h: Z[h % 2]})
                            sb_log(i - 1, [h])
                        h, step = divmod(ub - 6, 4)
                        if ub >= 6 and step == 0 and h < GH:
                            sb_weights(i - 1, h, Z[h % 2])
                        h, step = divmod(ub - 9, 4)
                        if ub >= 9 and step == 0 and h < GH:
                            sb_out(i - 1, h, 1, YB[h % 2])
                    if ub == 19:
                        act.wait_ge(turned, i * 4 + 1)
                        nc.scalar.activation(qT[:, 0:2, :], TRB[0][:, :].rearrange("p (h n) -> p h n", h=2), ACT.Copy,
                                             scale=SCALE).then_inc(turned_act, 1)
                    if ub == 22:
                        act.wait_ge(turned, i * 4 + 3)
                        nc.scalar.activation(kT[:, 0:2, :], TRB[0][:, :].rearrange("p (h n) -> p h n", h=2),
                                             ACT.Copy).then_inc(turned_act, 1)

            sb_body(0, True)
            with act.Fori(1, GROUPS) as i:
                sb_body(i, False)

            def rest(ph):
                with act.Fori(1, ph.bodies) as c:
                    for ub in range(ph.nb):
                        split(ph, c, ub, False)

            last = GROUPS - 1
            for ub in range(PB.nb):
                split(PB, 0, ub, True)
                if ub == 2:
                    stage(PB.c0 - 1, sv, COLS, sb_free)
                    sb_abs_exp(last, range(GH), Z4)
                if ub == 3:
                    sb_log(last, range(GH))
                if ub == 4:
                    for h in range(GH):
                        sb_weights(last, h, Z4[h])
                if ub == 6:
                    sb_out(last, 0, 2, MAIN[0])
                    sb_out(last, 2, 2, MAIN[1])
            rest(PB)

            def ht_hi(l, c):
                for r in range(2):
                    act.wait_ge(h_turned[l], c * 2 + r + 1)
                    nc.scalar.activation(arena_hi[:, bass.ds(c * 4 + 2 * r, 2), :],
                                         TRB[r][:, :].rearrange("p (k n) -> p k n", k=2),
                                         ACT.Copy).then_inc(ht_hi_done[l], 1)

            def pair(ph, l, ev, c, first):
                for ub in range(ph.nb):
                    if first:
                        x_before(ev, ub)
                    split(ph, c, ub, first)
                    if ub == 7 and not first:
                        ht_hi(l, c - 1)
                    if ub == (10 if first else 9):
                        if first:
                            act.wait_ge(xt_lo_done, 8 * ev + KT // 2)
                        else:
                            act.wait_ge(h_turned[l], c * 2)
                        for tt in range(TT):
                            if tt == 0:
                                act.wait_ge(tt0_done, c * 2 + ph.c0 + 1)
                            else:
                                act.wait_ge(unit_used, ph.unit(c, ph.n))
                            nc.scalar.activation(stg[:, tt, :], MAIN[tt][:, :], ACT.Silu).then_inc(silu_done[l], 1)

            def swiglu(pg, pd, l):
                ev = 2 * l + 1
                pair(pg, l, ev, 0, True)
                with act.Fori(1, PAIRS) as c:
                    pair(pg, l, ev, c, False)
                for ub in range(pd.nb):
                    split(pd, 0, ub, True)
                    if ub == 6:
                        ht_hi(l, PAIRS - 1)
                rest(pd)

            act.wait_ge(gbT_ready, 1)
            swiglu(PC, PD, 0)

            def d_steps(ub, h, pos, second, third):
                if ub == pos["exp"]:
                    for t, cols in ((0, slice(0, G * P)), (1, slice(G * P, SC))):
                        act.wait_ge(max_done, h * 2 + t + 1)
                        nc.scalar.activation(sm[:, cols], sm[:, cols], ACT.Exp, bias=mx[:, t:t + 1],
                                             accum_out=den[:, t:t + 1]).then_inc(p_done, 1)
                for g in (0, 2):
                    if ub == pos["take" if g == 0 else "take2"]:
                        act.wait_ge(p_turned, h * 3 + g + 1)
                        nc.scalar.activation(pT[:, g, :], TRB[0][:, 0:TRI], ACT.Copy).then_inc(pT_act, 1)
                if ub == pos["hi"]:
                    act.wait_ge(do_done, h * 2 + 1)
                    nc.scalar.activation(ot_hi[:, bass.ds(h * G, 2), :],
                                         second[:, :].rearrange("p (k n) -> p k n", k=2), ACT.Copy).then_inc(do_hi_done, 1)
                    act.wait_ge(do_done, h * 2 + 2)
                    nc.scalar.activation(ot_hi[:, bass.ds(h * G + 2, 1), :].rearrange("p a n -> p (a n)"),
                                         third[:, 0:SEQ], ACT.Copy).then_inc(do_hi_done, 1)

            def d_body(i, first):
                for ub in range(PE_.nb):
                    if first:
                        x_before(2, ub)
                    split(PE_, i, ub, first)
                    if ub == (10 if first else 8):
                        stage(i * 3 + PE_.c0, dq, GC, d_free)
                    if ub == 16:
                        stage(i * 3 + (PE_.c0 + 1), dk, GC, d_free)
                    if not first:
                        if ub == 1:
                            stage(i * 3 + (PE_.c0 - 1), dv, GC, d_free)
                        d_steps(ub, i - 1, IN_BODY, YB[1], YB[0])
                    if ub == 19:
                        act.wait_ge(d_turned, i * 4 + 1)
                        nc.scalar.activation(dqT[:, 0:2, :], TRB[0][:, :].rearrange("p (h n) -> p h n", h=2),
                                             ACT.Copy).then_inc(d_turned_act, 1)
                    if ub == 23:
                        act.wait_ge(d_turned, i * 4 + 3)
                        nc.scalar.activation(dkT[:, 0:2, :], TRB[0][:, :].rearrange("p (h n) -> p h n", h=2),
                                             ACT.Copy).then_inc(d_turned_act, 1)

            d_body(0, True)
            with act.Fori(1, HPG) as i:
                d_body(i, False)
            for ub in range(PF.nb):
                split(PF, 0, ub, True)
                if ub == 1:
                    stage(PF.c0 - 1, dv, GC, d_free)
                d_steps(ub, HPG - 1, AT_END, MAIN[0], MAIN[1])
            rest(PF)

            swiglu(PG, PH, 1)

        @block.vector
        def _(dve):
            def split(ph, body, ub):
                u = ub % ph.n
                l = ph.load[u]
                dve.wait_ge(hi_done, ph.unit(body, ub) + 1)
                at, n = (ph.k0[u] - ph.k0[ph.first_of[l]]) * ph.ncols, ph.nk[u] * ph.ncols
                nc.vector.tensor_tensor(w_lo[:, ph.slot[u], 0:n], raw[:, l % SLOTS, at:at + n],
                                        w_hi[:, ph.slot[u], 0:n].bitcast(F32), ALU.subtract).then_inc(lo_done, 1)

            def norm(ln, q):
                for tt in range(TT):
                    part = resid[:, tt, q * COLS:(q + 1) * COLS]
                    nc.vector.tensor_scalar(part, part, mv[:, tt, 0:1], rstd[:, tt:tt + 1], ALU.subtract,
                                            ALU.mult).then_inc(normed, 1)

            def y_add(ph, ln, c, tt):
                if tt == 0:
                    dve.wait_ge(tt0_done, c + (ph.c0 + 1))
                else:
                    dve.wait_ge(unit_used, ph.unit(c, ph.n))
                part = resid[:, tt, bass.ds(c * COLS, COLS)]
                nc.vector.scalar_tensor_tensor(out=part, in0=part, scalar=ALPHA, in1=YB[tt][:, :], op0=ALU.mult,
                                               op1=ALU.add).then_inc(y_added, 1)

            def y_stat(ln, c, tt):
                dve.wait_ge(y_added, c * 2 + (8 * ln + tt + 1))
                nc.vector.bn_stats(stats[:, tt, bass.ds(c, 1), :].rearrange("p a s -> p (a s)"),
                                   resid[:, tt, bass.ds(c * COLS, COLS)]).then_inc(y_stats, 1)

            def y_take(ph, ln, c):
                for tt in range(TT):
                    y_add(ph, ln, c, tt)
                    y_stat(ln, c, tt)

            def moments(ln):
                dve.wait_ge(y_stats, 8 * (ln + 1))
                for tt in range(TT):
                    nc.vector.bn_aggr(mv[:, tt, :], stats[:, tt, :, :].rearrange("p c s -> p (c s)")).then_inc(ln_mean, 1)
                dve.wait_ge(ln_mean, 2 * (ln + 1))
                nc.vector.tensor_scalar(veps[:, :], mv[:, :, 1], EPS, None, ALU.add).then_inc(ln_veps, 1)

            def x_before(ev, ub):
                if ub == 2 and ev > 0:
                    moments(ev - 1)
                    dve.wait_ge(ln_rstd, ev)
                    norm(ev - 1, 0)
                    norm(ev - 1, 1)
                for r in x_rounds(ev, ub):
                    two = stg[:, r % 2, :].rearrange("p (k n) -> p k n", k=2)
                    dve.wait_ge(xt_read, 8 * ev + r + 1)
                    nc.vector.tensor_copy(xt_hi[:, 2 * r:2 * r + 2, :], two).then_inc(xt_hi_done, 1)
                    dve.wait_ge(xt_hi_done, 8 * ev + r + 1)
                    nc.vector.tensor_tensor(xt_lo[:, 2 * r:2 * r + 2, :], two,
                                            xt_hi[:, 2 * r:2 * r + 2, :].bitcast(F32), ALU.subtract).then_inc(xt_lo_done, 1)
                    if ev > 0 and r in (0, 2):
                        norm(ev - 1, r // 2 + 2)

            def stage(units, dst, width, free):
                dve.wait_ge(unit_used, units)
                nc.vector.tensor_copy(dst[:, 1, :], MAIN[1][:, 0:width]).then_inc(free[1], 1)

            def sb_stay(g, h, z):
                dve.wait_ge(log_done, g * GH + h + 1)
                nc.vector.scalar_tensor_tensor(out=s_buf[:, h, :], in0=z[:, 0:TRI], scalar=0.0,
                                               in1=ew_buf[:, h, :], op0=ALU.max, op1=ALU.add).then_inc(stay_done, 1)

            def sb_out(g, h, n, bank):
                dve.wait_ge(o_hi_done, g * GH + h + n)
                heads = bass.ds(g * GH + h, n)
                nc.vector.tensor_tensor(ot_lo[:, heads, :], bank[:, 0:n * SEQ].rearrange("p (a t) -> p a t", a=n),
                                        ot_hi[:, heads, :].bitcast(F32), ALU.subtract).then_inc(o_free, n)

            def sb_body(i, first):
                for ub in range(PA.nb):
                    if first:
                        x_before(0, ub)
                    split(PA, i, ub)
                    if not first:
                        if ub == 1:
                            stage(PA.unit(i, 0), sv, COLS, sb_free)
                        h, step = divmod(ub - 4, 4)
                        if ub >= 4 and step == 0 and h < GH:
                            sb_stay(i - 1, h, Z[h % 2])
                        h, step = divmod(ub - 10, 4)
                        if ub >= 10 and step == 0 and h < GH:
                            sb_out(i - 1, h, 1, YB[h % 2])
                    if ub == (10 if first else 8):
                        stage(PA.unit(i, PA.n), sq, COLS, sb_free)
                    if ub == 16:
                        stage(PA.unit(i, 2 * PA.n), sk, COLS, sb_free)
                    if ub == 19:
                        dve.wait_ge(turned, i * 4 + 2)
                        nc.vector.tensor_scalar(qT[:, 2:4, :], TRB[1][:, :].rearrange("p (h n) -> p h n", h=2), SCALE, None,
                                                ALU.mult).then_inc(turned_dve, 1)
                    if ub == 22:
                        dve.wait_ge(turned, i * 4 + 4)
                        nc.vector.tensor_copy(kT[:, 2:4, :], TRB[1][:, :].rearrange("p (h n) -> p h n", h=2)).then_inc(
                            turned_dve, 1)

            for free, small in ((o_free, mx), (do_lo_done, rden), (ht_lo_done[0], veps), (ht_lo_done[1], mv[:, 0, :])):
                nc.vector.memset(small[:, :], 0.0).then_inc(free, FREE)
            sb_body(0, True)
            with dve.Fori(1, GROUPS) as i:
                sb_body(i, False)

            def y_rest(ph, ln):
                if ln > 0:
                    dve.wait_ge(resid_done, 8 * ln)
                with dve.Fori(1, OUTC) as c:
                    for ub in range(ph.nb):
                        split(ph, c, ub)
                        for tt in range(TT):
                            if ub == 0:
                                y_add(ph, ln, c - 1, tt)
                            if ub == 1:
                                y_stat(ln, c - 1, tt)

            last = GROUPS - 1
            for ub in range(PB.nb):
                split(PB, 0, ub)
                if ub == 2:
                    stage(PB.u0, sv, COLS, sb_free)
                if ub == 3:
                    for h in range(GH):
                        sb_stay(last, h, Z4[h])
                if ub == 6:
                    sb_out(last, 0, 2, MAIN[0])
                    sb_out(last, 2, 2, MAIN[1])
            y_rest(PB, 0)

            def h_take(ph, l, c):
                for tt in range(TT):
                    dve.wait_ge(silu_done[l], c * 2 + tt + 1)
                    if tt == 0:
                        dve.wait_ge(tt0_done, c * 2 + ph.c0 + 2)
                    else:
                        dve.wait_ge(unit_used, ph.unit(c, ph.nb))
                    nc.vector.tensor_tensor(stg[:, tt, :], stg[:, tt, :], UP[tt][:, :], ALU.mult).then_inc(h_done[l], 1)

            def ht_lo(l, c):
                for r in range(2):
                    dve.wait_ge(ht_hi_done[l], c * 2 + r + 1)
                    tiles = bass.ds(c * 4 + 2 * r, 2)
                    nc.vector.tensor_tensor(arena_lo[:, tiles, :], TRB[r][:, :].rearrange("p (k n) -> p k n", k=2),
                                            arena_hi[:, tiles, :].bitcast(F32), ALU.subtract).then_inc(ht_lo_done[l], 1)

            def pair(pd_before, ph, l, ev, c, first):
                for ub in range(ph.nb):
                    if first:
                        if ub == 2:
                            y_take(pd_before, ev - 1, OUTC - 1)
                        x_before(ev, ub)
                    split(ph, c, ub)
                    if not first:
                        if ub == 1:
                            h_take(ph, l, c - 1)
                        if ub == 8:
                            ht_lo(l, c - 1)

            def swiglu(before, pg, pd, l):
                ev = 2 * l + 1
                pair(before, pg, l, ev, 0, True)
                dve.wait_ge(resid_done, 8 * ev)
                with dve.Fori(1, PAIRS) as c:
                    pair(before, pg, l, ev, c, False)
                for ub in range(pd.nb):
                    split(pd, 0, ub)
                    if ub == 1:
                        h_take(pg, l, PAIRS - 1)
                    if ub == 7:
                        ht_lo(l, PAIRS - 1)
                y_rest(pd, ev)

            swiglu(PB, PC, PD, 0)

            def rope_half(i, part, tt, dst):
                dve.wait_ge(d_free[tt], i * 3 + (part + 1))
                src = dst[:, tt, :].rearrange("p (g d) -> p g d", g=G)
                a = rope_a[:, tt, :].rearrange("p (g d) -> p g d", g=G)
                b = rope_b[:, tt, :].rearrange("p (g d) -> p g d", g=G)
                H2 = HD // 2
                cos = cs_tab[:, tt, 0, :].unsqueeze(1).to_broadcast((P, G, HD))
                sin = cs_tab[:, tt, 1, :].unsqueeze(1).to_broadcast((P, G, HD))
                nc.vector.tensor_tensor(a, src, cos, ALU.mult).then_inc(rope_parts, 1)
                nc.vector.tensor_tensor(b[:, :, 0:H2], src[:, :, H2:HD], sin[:, :, 0:H2], ALU.mult).then_inc(rope_parts, 1)
                nc.vector.tensor_tensor(b[:, :, H2:HD], src[:, :, 0:H2], sin[:, :, H2:HD], ALU.mult).then_inc(rope_parts, 1)
                dve.wait_ge(rope_parts, i * 12 + (2 * part + tt + 1) * 3)
                nc.vector.tensor_tensor(src, a, b, ALU.add).then_inc(roped, 1)

            def d_steps(ub, h, pos, second, third):
                if ub == pos["mask"]:
                    dve.wait_ge(scores_done, h + 1)
                    for src, n, at in ((Z[0], G * P, 0), (Z[1], 2 * SEQ, G * P), (third, SEQ, G * P + 2 * SEQ)):
                        nc.vector.scalar_tensor_tensor(out=sm[:, at:at + n], in0=src[:, 0:n], scalar=SCALE,
                                                       in1=mask_sb[:, at:at + n], op0=ALU.mult,
                                                       op1=ALU.add).then_inc(scores_masked, 1)
                if ub == pos["top"]:
                    dve.wait_ge(scores_masked, h * 3 + 3)
                    for t, cols in ((0, slice(0, G * P)), (1, slice(G * P, SC))):
                        nc.vector.tensor_reduce(mx[:, t:t + 1], sm[:, cols], AX.X, ALU.max, negate=True).then_inc(max_done, 1)
                if ub == pos["norm"]:
                    dve.wait_ge(p_done, h * 2 + 2)
                    nc.vector.reciprocal(rden[:, :], den[:, :]).then_inc(rden_done, 1)
                    dve.wait_ge(rden_done, h + 1)
                    for t, cols in ((0, slice(0, G * P)), (1, slice(G * P, SC))):
                        nc.vector.tensor_scalar(sm[:, cols], sm[:, cols], rden[:, t:t + 1], None,
                                                ALU.mult).then_inc(p_scaled, 1)
                if ub == pos["take"]:
                    dve.wait_ge(p_turned, h * 3 + 2)
                    nc.vector.tensor_copy(pT[:, 1, :], TRB[1][:, 0:TRI]).then_inc(pT_dve, 1)
                if ub == pos["lo"]:
                    dve.wait_ge(do_hi_done, h * 2 + 1)
                    two = bass.ds(h * G, 2)
                    nc.vector.tensor_tensor(ot_lo[:, two, :], second[:, :].rearrange("p (k n) -> p k n", k=2),
                                            ot_hi[:, two, :].bitcast(F32), ALU.subtract).then_inc(do_lo_done, 1)
                    dve.wait_ge(do_hi_done, h * 2 + 2)
                    one = bass.ds(h * G + 2, 1)
                    nc.vector.tensor_tensor(ot_lo[:, one, :].rearrange("p a n -> p (a n)"), third[:, 0:SEQ],
                                            ot_hi[:, one, :].rearrange("p a n -> p (a n)").bitcast(F32),
                                            ALU.subtract).then_inc(do_lo_done, 1)

            def d_body(i, first):
                for ub in range(PE_.nb):
                    if first:
                        if ub == 2:
                            y_take(PD, 1, OUTC - 1)
                        x_before(2, ub)
                    split(PE_, i, ub)
                    if not first:
                        if ub == 1:
                            stage(PE_.unit(i, 0), dv, GC, d_free)
                        d_steps(ub, i - 1, IN_BODY, YB[1], YB[0])
                    if ub == (10 if first else 8):
                        stage(PE_.unit(i, PE_.n), dq, GC, d_free)
                    if ub == 16:
                        stage(PE_.unit(i, 2 * PE_.n), dk, GC, d_free)
                    if first and ub == 10:
                        dve.wait_ge(tables_in, 32)
                    for part, dst in ((0, dq), (1, dk)):
                        for tt in range(TT):
                            if ub == 8 * part + 10 + tt:
                                rope_half(i, part, tt, dst)
                    if ub == 19:
                        dve.wait_ge(d_turned, i * 4 + 2)
                        nc.vector.tensor_copy(dqT[:, 2, :], TRB[1][:, 0:SEQ]).then_inc(d_turned_dve, 1)
                    if ub == 23:
                        dve.wait_ge(d_turned, i * 4 + 4)
                        nc.vector.tensor_copy(dkT[:, 2, :], TRB[1][:, 0:SEQ]).then_inc(d_turned_dve, 1)

            d_body(0, True)
            with dve.Fori(1, HPG) as i:
                d_body(i, False)
            for ub in range(PF.nb):
                split(PF, 0, ub)
                if ub == 1:
                    stage(PF.u0, dv, GC, d_free)
                d_steps(ub, HPG - 1, AT_END, MAIN[0], MAIN[1])
            y_rest(PF, 2)

            swiglu(PF, PG, PH, 1)

            y_take(PH, 3, OUTC - 1)
            moments(3)
            dve.wait_ge(gb_in, 32 * 4)

            def out_piece(n):
                return n % TT, slice(n // TT * COLS, (n // TT + 1) * COLS), slice(D + n // TT * COLS, D + (n // TT + 1) * COLS)

            def centre(n):
                tt, cols, _ = out_piece(n)
                nc.vector.scalar_tensor_tensor(out=resid[:, tt, cols], in0=resid[:, tt, cols], scalar=mv[:, tt, 0:1],
                                               in1=gb_last[:, cols], op0=ALU.subtract, op1=ALU.mult).then_inc(out_scaled, 1)

            def finish(n):
                tt, cols, bias = out_piece(n)
                dve.wait_ge(out_scaled, n - POOL_PIECES + 1)
                nc.vector.scalar_tensor_tensor(out=resid[:, tt, cols], in0=resid[:, tt, cols], scalar=rstd[:, tt:tt + 1],
                                               in1=gb_last[:, bias], op0=ALU.mult, op1=ALU.add).then_inc(out_ready, 1)

            centre(POOL_PIECES)
            centre(POOL_PIECES + 1)
            dve.wait_ge(ln_rstd, 4)
            for n in range(POOL_PIECES):
                tt, cols, _ = out_piece(n)
                nc.vector.tensor_scalar(resid[:, tt, cols], resid[:, tt, cols], mv[:, tt, 0:1], rstd[:, tt:tt + 1],
                                        ALU.subtract, ALU.mult).then_inc(normed, 1)
            for n in range(POOL_PIECES, PIECES):
                finish(n)
                if n + 2 < PIECES:
                    centre(n + 2)

        @block.gpsimd
        def _(pool):
            def gb_load(ln, dst):
                for v, row in enumerate(gb_rows_of(ln)):
                    pool.dma_start(dst[:, v * D:(v + 1) * D], row.to_broadcast((P, D))).then_inc(gb_in, 16)

            def causal(buf, head, wait, value, done):
                pool.wait_ge(wait, value)
                v = buf[:, head, :].rearrange("p (b t) -> p b t", b=3)[:, 0:3:2, :]
                nc.gpsimd.affine_select(out=v, in_=v, compare_op=ALU.is_gt, fill=0.0, base=0, pattern=[[0, 2], [1, P]],
                                        channel_multiplier=-1).then_inc(done, 1)

            def sb_masks(g, heads):
                for h in heads:
                    causal(s_buf, h, stay_done, g * GH + h + 1, stay_masked)
                    causal(ew_buf, h, w_done, g * GH + h + 1, w_masked)

            def inv_sqrt(ln):
                pool.wait_ge(ln_veps, ln + 1)
                nc.gpsimd.tensor_tensor(rstd[:, :], veps[:, :], half[:, :], ALU.pow).then_inc(ln_rstd, 1)

            def residual(ln):
                pool.wait_ge(gb_in, 32 * (ln + 1))
                for q in range(OUTC):
                    pool.wait_ge(xt_turned, 8 * (ln + 1) + 2 * q + 2)
                    for tt in range(TT):
                        n = 8 * ln + TT * q + tt
                        part = resid[:, tt, q * COLS:(q + 1) * COLS]
                        nc.gpsimd.tensor_tensor(part, part, gb_flat[:, q * COLS:(q + 1) * COLS], ALU.mult).then_inc(scaled, 1)
                        pool.wait_ge(scaled, n + 1)
                        nc.gpsimd.tensor_tensor(part, part, gb_flat[:, D + q * COLS:D + (q + 1) * COLS],
                                                ALU.add).then_inc(resid_done, 1)

            nc.gpsimd.memset(half[:, :], -0.5).then_inc(half_set, 1)
            pool.wait_ge(half_set, 1)
            pool.wait_ge(unit_used, PA.n)
            gb_load(0, gb_flat)
            for g in range(GROUPS - 1):
                sb_masks(g, range(GH))
            last = GROUPS - 1
            for h in range(GH):
                causal(s_buf, h, stay_done, GH * last + h + 1, stay_masked)
            for h in range(GH):
                causal(ew_buf, h, w_done, GH * last + h + 1, w_masked)
            inv_sqrt(0)
            residual(0)
            inv_sqrt(1)
            pool.wait_ge(unit_used, PE_.u0)
            gb_load(1, gb_flat)
            pool.dma_start(cs_tab, rope).then_inc(tables_in, 16)
            pool.dma_start(mask_sb, masks).then_inc(tables_in, 16)
            residual(1)
            pool.wait_ge(resid_done, 16)
            gb_load(2, gb_flat)
            inv_sqrt(2)
            residual(2)
            pool.wait_ge(unit_used, PH.u0)
            gb_load(3, gb_last)
            inv_sqrt(3)
            pool.wait_ge(gb_in, 32 * 4)
            for n in range(POOL_PIECES):
                cols = slice(n // TT * COLS, (n // TT + 1) * COLS)
                part = resid[:, n % TT, cols]
                pool.wait_ge(normed, 8 * 3 + n + 1)
                nc.gpsimd.tensor_tensor(part, part, gb_last[:, cols], ALU.mult).then_inc(out_scaled_pool, 1)
                pool.wait_ge(out_scaled_pool, n + 1)
                nc.gpsimd.tensor_tensor(part, part, gb_last[:, D + cols.start:D + cols.stop],
                                        ALU.add).then_inc(out_ready_pool, 1)


def shape_constants():
    j = np.arange(P)
    tri = np.stack([np.eye(P), -(j[:, None] >= j[None, :]).astype(float), -np.ones((P, P))], 1).astype(np.float32)
    pos = np.arange(SEQ, dtype=np.float32)
    inv = np.float32(THETA) ** (-np.arange(0, HD, 2, dtype=np.float32) / np.float32(HD))
    ang = pos[:, None] * inv[None, :]
    cos, sin = np.cos(ang), np.sin(ang)
    table = np.stack([np.concatenate([cos, cos], 1), np.concatenate([-sin, sin], 1)], 1)
    rope = np.ascontiguousarray(table.reshape(TT, P, 2, HD).transpose(1, 0, 2, 3)).astype(np.float32)
    blocks = []
    for t0, keys in ((0, P), (P, SEQ)):
        for window, dilation in DIL:
            back = (t0 + np.arange(P))[:, None] - np.arange(keys)[None, :]
            valid = (back >= 0) & (back % dilation == 0) & (back <= window)
            blocks.append(np.where(valid, 0.0, NEG))
    return tri, rope, np.concatenate(blocks, 1).astype(np.float32)


_INS = ["x", "w_qkv_sb", "w_o_sb", "w_qkv_dil", "w_o_dil", "ln_mix_g", "ln_mix_b", "w_gate_up", "w_down", "ln_ffn_g",
        "ln_ffn_b"]


def kernel(**inputs):
    import concourse.bacc as bacc
    from concourse.bass_utils import run_bass_kernel_spmd

    nc = bacc.Bacc("TRN2", target_bir_lowering=False, num_devices=1)
    arrays, args = {}, []
    tri, rope, masks = shape_constants()
    for name, a in [(n, np.ascontiguousarray(inputs[n])) for n in _INS] + [("tri", tri), ("rope", rope), ("masks", masks)]:
        arrays[f"in_{name}"] = a
        args.append(nc.dram_tensor(f"in_{name}", a.shape, mybir.dt.from_np(a.dtype), kind="ExternalInput").ap())
    args.append(nc.dram_tensor("out_0", (1, SEQ, D), F32, kind="ExternalOutput").ap())
    build(nc, *args)
    r = run_bass_kernel_spmd(nc, [arrays], core_ids=[0])
    return r.results[0]["out_0"]
```
